# Optimizing a Trainium2 kernel written in Bass

```python
import jax
import jax.numpy as jnp
from jax import lax
import numpy as np

D_MODEL = 1024
BATCH = 1
SEQ = 256
DEPTH = 2

GRID_W = 64
HEAD_DIM = 64
RMS_EPS = 1e-6
NEG_INF = -1e30
Q_BLOCK = 128

A_HEADS = 4
NA_ROWS_MAX = 8
NA_COLS = 16
B_HEADS = 4
DILATED_BRANCHES = ((128, 1), (512, 4), (2048, 16))
C_HEADS = 8
C_KV_HEADS = 2
ROPE_THETA = 10000.0

A_W = A_HEADS * HEAD_DIM
B_W = B_HEADS * HEAD_DIM
C_W = C_HEADS * HEAD_DIM
C_KV_W = C_KV_HEADS * HEAD_DIM
MIX_W = A_W + B_W + C_W
IN_SPLITS = (A_W, A_W, A_W, B_W, B_W, B_W, C_W, C_KV_W, C_KV_W)
IN_COLS = sum(IN_SPLITS)

N_GROUPS = 4
EXPERTS_PER_GROUP = 8
N_EXPERTS = N_GROUPS * EXPERTS_PER_GROUP
TOP_K_IN_GROUP = 2
D_EXPERT = 512
MOE_BLOCK = 256

kernel_name = "hybrid_na_dilated_gqa_hiermoe_encoder"

def rms_norm(x, g):
    xf = x.astype(jnp.float32)
    y = xf * lax.rsqrt(jnp.mean(xf * xf, axis=-1, keepdims=True) + RMS_EPS)
    return (y * g.astype(jnp.float32)).astype(x.dtype)

def alibi_slopes(n):
    return jnp.exp2(-8.0 * jnp.arange(1, n + 1, dtype=jnp.float32) / n)

def axial_rope(x):
    b, s, h, d = x.shape
    n_freq = d // 4
    t = jnp.arange(s)
    inv_freq = ROPE_THETA ** (-jnp.arange(n_freq, dtype=jnp.float32) / n_freq)
    rows = (t // GRID_W).astype(jnp.float32)
    cols = (t % GRID_W).astype(jnp.float32)
    ang = jnp.stack([rows[:, None] * inv_freq, cols[:, None] * inv_freq], axis=1)
    cos = jnp.cos(ang)[None, :, None]
    sin = jnp.sin(ang)[None, :, None]
    xr = x.astype(jnp.float32).reshape(b, s, h, 2, 2, n_freq)
    x1, x2 = xr[..., 0, :], xr[..., 1, :]
    out = jnp.stack([x1 * cos - x2 * sin, x2 * cos + x1 * sin], axis=-2)
    return out.reshape(b, s, h, d).astype(x.dtype)

def neighbourhood_attention(q, k, v, rpb):
    bsz, s, h, hd = q.shape
    rows = s // GRID_W
    kh = min(NA_ROWS_MAX, rows)
    scale = hd ** -0.5
    qg = q.reshape(bsz, rows, GRID_W, h, hd)
    kg = k.reshape(bsz, rows, GRID_W, h, hd)
    vg = v.reshape(bsz, rows, GRID_W, h, hd)
    cols = jnp.arange(GRID_W)
    col_start = jnp.clip(cols - NA_COLS // 2, 0, GRID_W - NA_COLS)
    col_idx = col_start[:, None] + jnp.arange(NA_COLS)[None, :]
    dc = col_idx - cols[:, None]

    def row_block(args):
        r, q_row = args
        r0 = jnp.clip(r - kh // 2, 0, rows - kh)
        k_rows = lax.dynamic_slice_in_dim(kg, r0, kh, axis=1)
        v_rows = lax.dynamic_slice_in_dim(vg, r0, kh, axis=1)
        k_nb = k_rows[:, :, col_idx]
        v_nb = v_rows[:, :, col_idx]
        sc = jnp.einsum('bqhd,bkqjhd->bhqkj', q_row, k_nb,
                        preferred_element_type=jnp.float32) * scale
        dr = r0 + jnp.arange(kh) - r
        bias = rpb[:, (dr + NA_ROWS_MAX - 1)[None, :, None], (dc + NA_COLS - 1)[:, None, :]]
        sc = sc + bias.astype(jnp.float32)[None]
        p = jax.nn.softmax(sc.reshape(bsz, h, GRID_W, kh * NA_COLS), axis=-1)
        p = p.reshape(bsz, h, GRID_W, kh, NA_COLS).astype(v.dtype)
        return jnp.einsum('bhqkj,bkqjhd->bqhd', p, v_nb)

    out = lax.map(row_block, (jnp.arange(rows), qg.transpose(1, 0, 2, 3, 4)))
    return out.transpose(1, 0, 2, 3, 4).reshape(bsz, s, h * hd)

def dilated_attention(q, k, v):
    bsz, s, h, hd = q.shape
    scale = hd ** -0.5
    slopes = alibi_slopes(h)
    n_blocks = s // Q_BLOCK
    qb = q.reshape(bsz, n_blocks, Q_BLOCK, h, hd).transpose(1, 0, 2, 3, 4)

    def block(args):
        i, q_blk = args
        pos = i * Q_BLOCK + jnp.arange(Q_BLOCK)
        maxes, dens, nums = [], [], []
        for window, dil in DILATED_BRANCHES:
            half = window // (2 * dil)
            offs = dil * jnp.arange(-half, half + 1)
            kp = pos[:, None] + offs[None, :]
            valid = (kp >= 0) & (kp < s)
            kpc = jnp.clip(kp, 0, s - 1)
            k_sel = jnp.take(k, kpc, axis=1)
            v_sel = jnp.take(v, kpc, axis=1)
            sc = jnp.einsum('bqhd,bqjhd->bhqj', q_blk, k_sel,
                            preferred_element_type=jnp.float32) * scale
            sc = sc - slopes[:, None, None] * jnp.abs(offs).astype(jnp.float32)[None, None, :]
            sc = jnp.where(valid[None, None], sc, NEG_INF)
            m = jnp.max(sc, axis=-1)
            p = jnp.exp(sc - m[..., None])
            maxes.append(m)
            dens.append(jnp.sum(p, axis=-1))
            nums.append(jnp.einsum('bhqj,bqjhd->bhqd', p, v_sel.astype(jnp.float32)))
        m_all = jnp.max(jnp.stack(maxes), axis=0)
        wts = [jnp.exp(m - m_all) for m in maxes]
        num = sum(w[..., None] * n for w, n in zip(wts, nums))
        den = sum(w * d for w, d in zip(wts, dens))
        o = num / den[..., None]
        return o.transpose(0, 2, 1, 3).astype(q.dtype)

    out = lax.map(block, (jnp.arange(n_blocks), qb))
    return out.transpose(1, 0, 2, 3, 4).reshape(bsz, s, h * hd)

def gqa_attention(q, k, v):
    bsz, s, hq, hd = q.shape
    hkv = k.shape[2]
    grp = hq // hkv
    scale = hd ** -0.5
    n_blocks = s // Q_BLOCK
    qb = q.reshape(bsz, n_blocks, Q_BLOCK, hkv, grp, hd).transpose(1, 0, 2, 3, 4, 5)

    def block(q_blk):
        sc = jnp.einsum('bqkgd,bskd->bkgqs', q_blk, k,
                        preferred_element_type=jnp.float32) * scale
        p = jax.nn.softmax(sc, axis=-1).astype(v.dtype)
        return jnp.einsum('bkgqs,bskd->bqkgd', p, v)

    out = lax.map(block, qb)
    return out.transpose(1, 0, 2, 3, 4, 5).reshape(bsz, s, hq * hd)

def mixer_sublayer(x, norm_g, w_in, qk_g, rpb, mix_g, w_out):
    bsz, s, _ = x.shape
    h = rms_norm(x, norm_g)
    proj = h @ w_in
    qa, ka, va, qb, kb, vb, qc, kc, vc = jnp.split(proj, list(np.cumsum(IN_SPLITS)[:-1]), axis=-1)

    def heads(t):
        return t.reshape(bsz, s, t.shape[-1] // HEAD_DIM, HEAD_DIM)

    qa = rms_norm(heads(qa), qk_g[0, 0])
    ka = rms_norm(heads(ka), qk_g[0, 1])
    qb = rms_norm(heads(qb), qk_g[1, 0])
    kb = rms_norm(heads(kb), qk_g[1, 1])
    qc = axial_rope(rms_norm(heads(qc), qk_g[2, 0]))
    kc = axial_rope(rms_norm(heads(kc), qk_g[2, 1]))

    oa = neighbourhood_attention(qa, ka, heads(va), rpb)
    ob = dilated_attention(qb, kb, heads(vb))
    oc = gqa_attention(qc, kc, heads(vc))

    merged = jnp.concatenate([
        rms_norm(oa, mix_g[:A_W]),
        rms_norm(ob, mix_g[A_W:A_W + B_W]),
        rms_norm(oc, mix_g[A_W + B_W:]),
    ], axis=-1)
    return merged @ w_out

def hier_moe(h, w_rg, b_rg, w_re, b_re, w_gate, w_up, w_down):
    bsz, s, d = h.shape
    n = bsz * s
    xt = h.reshape(n, d)
    g_logits = jnp.dot(xt, w_rg, preferred_element_type=jnp.float32) + b_rg.astype(jnp.float32)
    g_prob = jax.nn.softmax(g_logits, axis=-1)
    grp = jnp.argmax(g_logits, axis=-1)
    p_grp = jnp.take_along_axis(g_prob, grp[:, None], axis=1)[:, 0]
    e_logits = (jnp.dot(xt, w_re, preferred_element_type=jnp.float32)
                + b_re.astype(jnp.float32)).reshape(n, N_GROUPS, EXPERTS_PER_GROUP)
    e_in = jnp.take_along_axis(e_logits, grp[:, None, None], axis=1)[:, 0]
    top_v, top_i = lax.top_k(e_in, TOP_K_IN_GROUP)
    gate = p_grp[:, None] * jax.nn.softmax(top_v, axis=-1)

    eid = (grp[:, None] * EXPERTS_PER_GROUP + top_i).reshape(-1).astype(jnp.int32)
    tok = jnp.repeat(jnp.arange(n, dtype=jnp.int32), TOP_K_IN_GROUP)
    wgt = gate.reshape(-1).astype(h.dtype)
    n_pairs = n * TOP_K_IN_GROUP
    cap = n_pairs + N_EXPERTS * MOE_BLOCK
    n_blk = cap // MOE_BLOCK

    order = jnp.argsort(eid)
    e_sorted = eid[order]
    counts = jnp.bincount(eid, length=N_EXPERTS)
    starts = jnp.cumsum(counts) - counts
    padded = (counts + MOE_BLOCK - 1) // MOE_BLOCK * MOE_BLOCK
    p_ends = jnp.cumsum(padded)
    p_starts = p_ends - padded
    dest = p_starts[e_sorted] + jnp.arange(n_pairs, dtype=jnp.int32) - starts[e_sorted]
    slot_tok = jnp.zeros((cap,), jnp.int32).at[dest].set(tok[order])
    slot_w = jnp.zeros((cap,), h.dtype).at[dest].set(wgt[order])
    blk_e = jnp.minimum(
        jnp.searchsorted(p_ends, jnp.arange(n_blk, dtype=jnp.int32) * MOE_BLOCK, side='right'),
        N_EXPERTS - 1)

    def expert_block(args):
        e, idx = args
        xb = xt[idx]
        return (jax.nn.silu(xb @ w_gate[e]) * (xb @ w_up[e])) @ w_down[e]

    y = lax.map(expert_block, (blk_e, slot_tok.reshape(n_blk, MOE_BLOCK))).reshape(cap, d)
    out = jnp.zeros_like(xt).at[slot_tok].add(y * slot_w[:, None])
    return out.reshape(bsz, s, d)

def setup_inputs(seed: int = 0) -> dict:
    key = jax.random.key(seed)
    ks = jax.random.split(key, 16)
    f32 = jnp.float32
    nrm = jax.random.normal
    return {
        "x": nrm(ks[0], (BATCH, SEQ, D_MODEL), f32),
        "norm1_g": 1.0 + 0.05 * nrm(ks[1], (DEPTH, D_MODEL), f32),
        "w_in": nrm(ks[2], (DEPTH, D_MODEL, IN_COLS), f32) * D_MODEL ** -0.5,
        "qk_norm_g": 1.0 + 0.05 * nrm(ks[3], (DEPTH, 3, 2, HEAD_DIM), f32),
        "na_rpb": 0.1 * nrm(ks[4], (DEPTH, A_HEADS, 2 * NA_ROWS_MAX - 1, 2 * NA_COLS - 1), f32),
        "mix_norm_g": 1.0 + 0.05 * nrm(ks[5], (DEPTH, MIX_W), f32),
        "w_out": nrm(ks[6], (DEPTH, MIX_W, D_MODEL), f32) * MIX_W ** -0.5,
        "norm2_g": 1.0 + 0.05 * nrm(ks[7], (DEPTH, D_MODEL), f32),
        "w_router_group": nrm(ks[8], (DEPTH, D_MODEL, N_GROUPS), f32) * D_MODEL ** -0.5,
        "b_router_group": 0.01 * nrm(ks[9], (DEPTH, N_GROUPS), f32),
        "w_router_expert": nrm(ks[10], (DEPTH, D_MODEL, N_EXPERTS), f32) * D_MODEL ** -0.5,
        "b_router_expert": 0.01 * nrm(ks[11], (DEPTH, N_EXPERTS), f32),
        "w_gate": nrm(ks[12], (DEPTH, N_EXPERTS, D_MODEL, D_EXPERT), f32) * D_MODEL ** -0.5,
        "w_up": nrm(ks[13], (DEPTH, N_EXPERTS, D_MODEL, D_EXPERT), f32) * D_MODEL ** -0.5,
        "w_down": nrm(ks[14], (DEPTH, N_EXPERTS, D_EXPERT, D_MODEL), f32) * D_EXPERT ** -0.5,
    }

def reference(x, norm1_g, w_in, qk_norm_g, na_rpb, mix_norm_g, w_out, norm2_g,
              w_router_group, b_router_group, w_router_expert, b_router_expert,
              w_gate, w_up, w_down):
    for l in range(DEPTH):
        x = x + mixer_sublayer(x, norm1_g[l], w_in[l], qk_norm_g[l], na_rpb[l],
                               mix_norm_g[l], w_out[l])
        x = x + hier_moe(rms_norm(x, norm2_g[l]), w_router_group[l], b_router_group[l],
                         w_router_expert[l], b_router_expert[l],
                         w_gate[l], w_up[l], w_down[l])
    return x


_drawn_inputs = setup_inputs


def setup_inputs(seed=0):
    import zlib

    import numpy as np

    out = dict(_drawn_inputs(seed))
    spreads = {}
    factors = {'b_router_group': 5.938, 'b_router_expert': 3.823}
    for name, (base, spread) in spreads.items():
        noise = np.random.default_rng([zlib.crc32(name.encode()), seed]).standard_normal(out[name].shape)
        drawn = base * np.exp(spread * noise) if base else spread * noise
        out[name] = jnp.asarray(drawn.astype(out[name].dtype))
    for name, factor in factors.items():
        out[name] = (out[name] * factor).astype(out[name].dtype)
    return out
```

```python
from contextlib import ExitStack

import numpy as np

import concourse.bass as bass
from concourse import mybir

F32 = mybir.dt.float32
BF16 = mybir.dt.bfloat16
I32 = mybir.dt.int32
ALU = mybir.AluOpType
ACT = mybir.ActivationFunctionType
AX_X = mybir.AxisListType.X

P = 128
LAYERS = 2
SEQ, D = 256, 1024
TT = SEQ // P
KD = D // P
HD = 64
IN_COLS = 2304
EPS = 1e-6
BIG = 1e30
GRID = 64
SCALE = HD ** -0.5

SEG = {"A": (0, 256, 512, 4, 4), "B": (768, 1024, 1280, 4, 4), "C": (1536, 2048, 2176, 8, 2)}
HEAD0 = {"A": 0, "B": 8, "C": 16}
NHEAD = 26
PAIRS = 8
KEYPAIR = [0, 1, 2, 3, 4, 4, 5, 5]

NG, NE, EPG = 4, 32, 8
DE = 512
KE = DE // P
CAP = 64
EPAIRS = NE // 2
PASSES = SEQ // CAP
UNROLL = 4
AHEAD = 3
SLOT = 8192
SLOTS = 4
MIX_USES = 1
MOE_USES = 3 * EPAIRS // SLOTS
USES = MIX_USES + MOE_USES

PROJ = TT * IN_COLS
KEYS = 6 * 2 * SEQ
WORK = PROJ + KEYS


def encoder(nc, a, out):
    ctx = ExitStack()
    with ctx:
        def sb(name, shape, dt=F32):
            return ctx.enter_context(nc.sbuf_tensor(name, shape, dt))

        def sem(name):
            return ctx.enter_context(nc.semaphore(name))

        ring = [sb(f"ring{i}", [P, SLOT]) for i in range(SLOTS)]
        x = sb("x", [P, TT, D])
        hn = sb("hn", [P, TT, D])
        hT = sb("hT", [P, KD, SEQ])
        work = sb("work", [P, WORK])
        rel = sb("rel", [P, 4, 7, GRID])
        dil = sb("dil", [P, 4, 3 * P])
        gain = sb("gain", [P, D])
        qkg = sb("qkg", [P, 6, HD])
        rope = sb("rope", [P, TT, 2, HD])
        colmask = sb("colmask", [P, GRID])
        ident = sb("ident", [P, P])
        tri = sb("tri", [P, P], BF16)
        ones = sb("ones", [P, P], BF16)
        iota = sb("iota", [P, SEQ])
        rev = sb("rev", [P, 36])
        w_route = sb("w_route", [P, KD, 36])
        b_route = sb("b_route", [P, 36])
        ms = sb("ms", [P, 8])
        rstd = sb("rstd", [P, 8])
        msh = sb("msh", [P, TT, NHEAD])
        rsh = sb("rsh", [P, TT, NHEAD])
        mhalf = sb("mhalf", [P, TT, NHEAD])
        eps = sb("eps", [P, TT, NHEAD])
        nmax = sb("nmax", [P, 2, 4])
        den = sb("den", [P, TT, 16])
        rden = sb("rden", [P, TT, 16])
        col = sb("col", [P, 12, TT])
        rg = sb("rg", [P, 2 * TT, NE + 2])
        rgc = sb("rgc", [P, 2 * TT, 2])
        flags = sb("flags", [1, EPAIRS * PASSES], I32)
        pairmax = sb("pairmax", [1, EPAIRS])
        mark = sb("mark", [1, 8])

        proj = work[:, 0:PROJ].rearrange("p (t c) -> p t c", t=TT)
        keys = work[:, PROJ:WORK].rearrange("p (j h s) -> p j h s", j=6, h=2)
        prob = [work[:, 0:512], work[:, 768:1280]]
        probT = [work[:, 1536:2048], work[:, IN_COLS:IN_COLS + 512]]
        o = [0]

        def carve(n):
            o[0] += n
            return work[:, o[0] - n:o[0]]

        xpart = carve(3 * TT * D // 2).bitcast(BF16).rearrange("p (i t k c) -> p i t k c", i=3, t=TT, k=KD)
        pick = carve(TT * P // 2).bitcast(BF16).rearrange("p (t s) -> p t s", t=TT)
        pickw = carve(TT * P).rearrange("p (t s) -> p t s", t=TT)
        pickT = carve(TT * P).rearrange("p (t s) -> p t s", t=TT)
        xg = carve(KD * P).rearrange("p (k s) -> p k s", k=KD)
        hid = carve(DE)
        hidT = carve(DE).rearrange("p (c s) -> p c s", c=KE)
        y = carve(D)
        lg, ra, rb = (carve(TT * 36).rearrange("p (t n) -> p t n", t=TT) for _ in range(3))
        oh1, oh2 = (carve(TT * NE).rearrange("p (t n) -> p t n", t=TT) for _ in range(2))
        chosen = carve(TT * NE // 2).bitcast(BF16).rearrange("p (t n) -> p t n", t=TT)
        relz = work[0:GRID, 0:28 * P].rearrange("p (n c) -> p n c", n=28)

        bank = [ctx.enter_context(nc.psum_tensor(f"bank{i}", [P, 512], F32)) for i in range(8)]
        skew = nc.dram_tensor("skew", (LAYERS, GRID * 28 * P), F32, kind="Internal").ap()

        d_x, d_const, d_rel0, d_skew, d_rel = sem("d_x"), sem("d_const"), sem("d_rel0"), sem("d_skew"), sem("d_rel")
        d_gain, d_small, d_out = sem("d_gain"), sem("d_small"), sem("d_out")
        landed = [sem(f"landed{i}") for i in range(SLOTS)]
        p_tr, p_proj, p_qk, p_s, p_pt, p_pv = (sem("p_" + n) for n in ("tr", "proj", "qk", "s", "pt", "pv"))
        p_out, p_logit, p_rank = sem("p_out"), sem("p_logit"), sem("p_rank")
        p_gather, p_gate, p_up, p_pickT, p_hidT, p_down, p_back = (
            sem("p_" + n) for n in ("gather", "gate", "up", "pickT", "hidT", "down", "back"))
        a_ss, a_hT, a_proj, a_sq, a_q, a_exp, a_pt = (sem("a_" + n) for n in ("ss", "hT", "proj", "sq", "q", "exp", "pt"))
        a_rexp, a_part, a_silu, a_pickT, a_xg, a_hidT, a_y = (
            sem("a_" + n) for n in ("rexp", "part", "silu", "pickT", "xg", "hidT", "y"))
        v_x, v_hn, v_hT, v_proj, v_ssh, v_qk, v_keys, v_soft = (
            sem("v_" + n) for n in ("x", "hn", "hT", "proj", "ssh", "qk", "keys", "soft"))
        v_o, v_router, v_chosen, v_flags, v_res, v_part, v_step = (
            sem("v_" + n) for n in ("o", "router", "chosen", "flags", "res", "part", "step"))
        v_pick, v_xg, v_hid, v_y, v_istep = (sem("v_" + n) for n in ("pick", "xg", "hid", "y", "istep"))
        v_back = [sem(f"v_back{n}") for n in range(4)]
        g_init, g_rstd, g_step, g_keys0, g_relz = sem("g_init"), sem("g_rstd"), sem("g_step"), sem("g_keys0"), sem("g_relz")
        seen = [sem(f"seen{i}") for i in range(5)]

        slot8 = [r[:, :].rearrange("p (k c) -> p k c", k=KD) for r in ring]
        slot_up = [r[:, :].rearrange("p (e k c) -> p e k c", e=2, k=KD) for r in ring]
        slot_dn = [r[:, :].rearrange("p (e k c) -> p e k c", e=2, k=KE) for r in ring]
        V_STEPS = 53

        def slot_of(i, j):
            u = 3 * i + j
            return u % SLOTS, u // SLOTS

        def run_layers(eng, extra, mixers, first, item, seen_sem):
            with eng.Fori(0, LAYERS) as l:
                e0 = eng.snap(extra, min_val=0, max_val=96)
                mixers(l, e0)
                first(eng.snap(l * (EPAIRS + 1) + e0, min_val=0, max_val=1000), 0, None)
                with eng.Fori(0, EPAIRS // UNROLL) as i4:
                    for ii in range(UNROLL):
                        q = eng.snap(l * EPAIRS + e0 + i4 * UNROLL + ii, min_val=0, max_val=1000)
                        so = [slot_of(ii, j) for j in range(3)]
                        rounds = [i4 * 3 + l * USES + (MIX_USES + r) + (e0 if s < 3 else 0) for s, r in so]
                        item(q, q + l, [s for s, _ in so], rounds, i4 * UNROLL + ii, True)
                eng.wait_ge(v_flags, l + 1)
                eng.sem_inc(seen_sem, 1)
                some = eng.value_load(flags[0:1, (PASSES - 1) * EPAIRS:(PASSES - 1) * EPAIRS + 1], min_val=0, max_val=1)
                with eng.If(some):
                    with eng.Fori(0, PASSES - 1) as ps:
                        with eng.Fori(0, EPAIRS) as pair:
                            again = eng.value_load(flags[0:1, bass.ds(ps * EPAIRS + pair, 1)], min_val=0, max_val=1)
                            with eng.If(again):
                                e = eng.snap(extra, min_val=0, max_val=96)
                                q = eng.snap(l * EPAIRS + EPAIRS + e, min_val=0, max_val=1000)
                                gq = eng.snap(q + l + 1, min_val=0, max_val=1000)
                                first(gq, pair, ps)
                                item(q, gq, [0, 1, 2], [l * USES + USES + e] * 3, pair, False)
                                eng.reg_add(extra, extra, 1)

        block = ctx.enter_context(nc.Block())

        @block.sync
        def _(sp):
            extra = sp.alloc_register("sp_extra")
            sp.reg_mov(extra, 0)
            xr = a["x"].rearrange("b (t p) d -> (b p) t d", t=TT)
            sp.dma_start(x[:, :, :], xr).then_inc(d_x, 16)

            def load_pair(pair, l, slots, free):
                for j, name in enumerate(("w_gate", "w_up", "w_down")):
                    s = slots[j]
                    free[j]()
                    k = KE if name == "w_down" else KD
                    src = a[name][bass.ds(l, 1), bass.ds(pair, 2)].rearrange("l e (p k) c -> p (l e) k c", k=k)
                    sp.dma_start(slot_dn[s] if name == "w_down" else slot_up[s], src).then_inc(landed[s], 16)

            with sp.Fori(0, LAYERS) as l:
                q0 = sp.snap(sp.snap(extra, min_val=0, max_val=96) + l * EPAIRS, min_val=0, max_val=1000)
                for s in range(3):
                    lo, hi = s * D, min(s * D + D, IN_COLS)
                    sp.wait_ge((p_gate, p_up, p_down)[s], q0 * (1, 1, 2)[s] + AHEAD)
                    src = a["w_in"][bass.ds(l, 1), :, lo:hi].rearrange("l (p k) c -> (l p) k c", k=KD)
                    sp.dma_start(slot8[s][:, :, 0:hi - lo], src).then_inc(landed[s], 16)
                sp.wait_ge(p_down, q0 * 2 + AHEAD)
                src = a["w_out"][bass.ds(l, 1)].rearrange("l (p k) c -> (l p) k c", k=KD)
                sp.dma_start(slot8[3], src).then_inc(landed[3], 16)
                with sp.Fori(0, EPAIRS // UNROLL) as i4:
                    q4 = sp.snap(q0 + i4 * UNROLL, min_val=0, max_val=1000)
                    for ii in range(UNROLL):
                        free = []
                        for j in range(3):
                            def wait(j=j):
                                before = 3 * ii + j - SLOTS
                                item, kind = before // 3, before % 3
                                per = (1, 1, 2)[kind]
                                value = sp.snap(q4 * per + ((item + 1) * per + AHEAD), min_val=1, max_val=2000)
                                if before < 0:
                                    s = 3 * ii + j
                                    if s < 3:
                                        sp.wait_ge(p_proj, 10 * l + (4, 8, 10)[s])
                                    else:
                                        sp.wait_ge(p_out, 4 * l + 4)
                                    sp.sem_inc(seen[0], 1)
                                sp.wait_ge((p_gate, p_up, p_down)[kind], value)
                            free.append(wait)
                        load_pair(i4 * (2 * UNROLL) + 2 * ii, l, [slot_of(ii, j)[0] for j in range(3)], free)
                sp.wait_ge(v_flags, l + 1)
                sp.sem_inc(seen[0], 1)
                some = sp.value_load(flags[0:1, (PASSES - 1) * EPAIRS:(PASSES - 1) * EPAIRS + 1], min_val=0, max_val=1)
                with sp.If(some):
                    with sp.Fori(0, PASSES - 1) as ps:
                        with sp.Fori(0, EPAIRS) as pair:
                            again = sp.value_load(flags[0:1, bass.ds(ps * EPAIRS + pair, 1)], min_val=0, max_val=1)
                            with sp.If(again):
                                q = sp.snap(sp.snap(extra, min_val=0, max_val=96) + (l + 1) * EPAIRS, min_val=0, max_val=1000)
                                load_pair(pair * 2, l, [0, 1, 2], [
                                    lambda: sp.wait_ge(p_gate, q + AHEAD), lambda: sp.wait_ge(p_up, q + AHEAD),
                                    lambda: sp.wait_ge(p_down, q * 2 + AHEAD)])
                                sp.reg_add(extra, extra, 1)
            sp.wait_ge(v_x, 2 * LAYERS + 1)
            sp.dma_start(out.rearrange("b (t p) d -> (b p) t d", t=TT), x[:, :, :]).then_inc(d_out, 16)
            sp.wait_ge(d_out, 16)

        @block.gpsimd
        def _(g):
            nc.gpsimd.memset(relz, 0.0).then_inc(g_relz, 1)
            for name, dst in (("c_rope", rope), ("c_colmask", colmask), ("c_ident", ident), ("c_dil", dil),
                              ("c_tri", tri), ("c_ones", ones), ("c_iota", iota), ("c_rev", rev)):
                g.dma_start(dst[:], a[name]).then_inc(d_const, 16)
            nc.gpsimd.memset(mhalf[:], -0.5).then_inc(g_init, 1)
            nc.gpsimd.memset(eps[:], EPS).then_inc(g_init, 1)
            for l in range(LAYERS):
                g.wait_ge(g_relz, 1)
                if l:
                    g.wait_ge(d_skew, 16 * l)
                src = a["na_rpb"][l, :, 4:11, :]
                for h in range(4):
                    s1 = src[h].partition_broadcast(GRID)
                    g.dma_start(relz[:, 7 * h:7 * h + 7, 48:79], s1).then_inc(d_rel0, 16)
                g.wait_ge(d_rel0, 64 * (l + 1))
                g.dma_start(skew[l].rearrange("(p m) -> p m", p=GRID), relz.rearrange("p n c -> p (n c)")).then_inc(d_skew, 16)
            g.wait_ge(d_skew, 16 * LAYERS)

            def root(n, width, dst, src, base):
                nc.gpsimd.tensor_tensor(src, src, eps[:].rearrange("p t h -> p (t h)")[:, 0:width], ALU.add).then_inc(g_step, 1)
                g.wait_ge(g_step, base)
                return nc.gpsimd.tensor_tensor(dst, src, mhalf[:].rearrange("p t h -> p (t h)")[:, 0:width], ALU.pow)

            g.wait_ge(g_init, 2)
            with g.Fori(0, LAYERS) as l:
                g.dma_start(gain[:], a["norm1_g"][bass.ds(l, 1), :].partition_broadcast(P).rearrange("p a c -> p (a c)")).then_inc(d_gain, 16)
                g.dma_start(qkg[:], a["qk_norm_g"][bass.ds(l, 1)].rearrange("l m q d -> l (m q) d").partition_broadcast(P).rearrange("p l m d -> p (l m) d")).then_inc(d_small, 16)
                g.dma_start(w_route[:, :, 0:NG], a["w_router_group"][bass.ds(l, 1)].rearrange("l (p k) n -> (l p) k n", k=KD)).then_inc(d_small, 16)
                g.dma_start(w_route[:, :, NG:36], a["w_router_expert"][bass.ds(l, 1)].rearrange("l (p k) n -> (l p) k n", k=KD)).then_inc(d_small, 16)
                g.dma_start(b_route[:, 0:NG], a["b_router_group"][bass.ds(l, 1), :].partition_broadcast(P).rearrange("p a c -> p (a c)")).then_inc(d_small, 16)
                g.dma_start(b_route[:, NG:36], a["b_router_expert"][bass.ds(l, 1), :].partition_broadcast(P).rearrange("p a c -> p (a c)")).then_inc(d_small, 16)
                pitch = 28 * P - 1
                rows = skew[bass.ds(l, 1), 63:63 + GRID * pitch].rearrange("l (c m) -> (l c) m", m=pitch)
                for half in range(2):
                    dst = rel[half * GRID:half * GRID + GRID].rearrange("p h r c -> p (h r) c")
                    g.dma_start(dst[:, 0:27, :], rows[:, 0:27 * P].rearrange("c (n k) -> c n k", k=P)[:, :, 0:GRID]).then_inc(d_rel, 16)
                    g.dma_start(dst[:, 27, :], rows[:, 27 * P:27 * P + GRID]).then_inc(d_rel, 16)
                g.wait_ge(a_ss, 3 * l + 1)
                root(2, TT, rstd[:, 0:TT], ms[:, 0:TT], 4 * l + 1).then_inc(g_rstd, 1)
                nc.gpsimd.memset(keys, 0.0).then_inc(g_keys0, 1)
                g.wait_ge(v_hn, 6 * l + 2)
                g.sem_inc(seen[4], 1)
                g.dma_start(gain[:], a["mix_norm_g"][bass.ds(l, 1), :].partition_broadcast(P).rearrange("p a c -> p (a c)")).then_inc(d_gain, 16)
                g.wait_ge(v_ssh, 6 * l + 6)
                root(1, TT * NHEAD, rsh[:].rearrange("p t h -> p (t h)"), msh[:].rearrange("p t h -> p (t h)"),
                     4 * l + 2).then_inc(g_rstd, 1)
                g.wait_ge(a_ss, 3 * l + 2)
                root(1, 6, rstd[:, 0:6], ms[:, 0:6], 4 * l + 3).then_inc(g_rstd, 1)
                g.wait_ge(v_hn, 6 * l + 4)
                g.sem_inc(seen[4], 1)
                g.dma_start(gain[:], a["norm2_g"][bass.ds(l, 1), :].partition_broadcast(P).rearrange("p a c -> p (a c)")).then_inc(d_gain, 16)
                g.wait_ge(a_ss, 3 * l + 3)
                root(1, TT, rstd[:, 0:TT], ms[:, 0:TT], 4 * l + 4).then_inc(g_rstd, 1)
                g.wait_ge(v_router, 2 * l + 2)

        GROUPS = ("A", "B", "C")
        hn_kc = hn[:].rearrange("p t (c k) -> p t k c", k=KD)
        queries = hT[:]
        BACK = [(0, 0), (1, 0), (0, 1), (1, 1)]

        @block.tensor
        def _(pe):
            extra = pe.alloc_register("pe_extra")
            pe.reg_mov(extra, 0)
            for s in (p_gather, p_gate, p_up, p_pickT, p_hidT, p_down, p_back):
                pe.sem_inc(s, AHEAD)
            pe.wait_ge(d_const, 16 * 8)

            def transposed_rows(l, n):
                pe.wait_ge(v_hn, 6 * l + 2 * n + 2)
                for j in range(4):
                    for kk in range(2):
                        for t in range(TT):
                            c = (2 * kk + t) * P
                            last = nc.tensor.transpose(bank[j][:, c:c + P], hn_kc[:, t, 2 * j + kk, :], ident[:])
                    last.then_inc(p_tr, 1)

            def rows_ready(l, n):
                pe.wait_ge(v_hT, 6 * l + 2 * n + 2)
                pe.wait_ge(a_hT, 6 * l + 2 * n + 2)

            def mixers(l, e0):
                transposed_rows(l, 0)
                rows_ready(l, 0)
                u = 0
                for s in range(3):
                    pe.wait_ge(landed[s], 16 * (l * USES + 1 + e0))
                    width = min(D, IN_COLS - s * D)
                    for c0 in range(0, width, 512):
                        w = min(512, width - c0)
                        for t in range(TT):
                            if u >= 4:
                                pe.wait_ge((v_proj, a_proj)[u % 2], 5 * l + (u - 4) // 2 + 1)
                            for k in range(KD):
                                last = nc.tensor.matmul(bank[4 + u % 4][:, 0:w], hT[:, k, t * P:t * P + P],
                                                        slot8[s][:, k, c0:c0 + w], start=(k == 0), stop=(k == KD - 1))
                            last.then_inc(p_proj, 1)
                            u += 1
                for gi, name in enumerate(GROUPS):
                    qo, ko, _, nq, nk = SEG[name]
                    pe.wait_ge(v_qk, 3 * l + gi + 1)
                    for b in range(nq // 4):
                        for pr in range(2):
                            for t in range(TT):
                                o0 = qo + (2 * b + pr) * P
                                c = (2 * pr + t) * P
                                last = nc.tensor.transpose(bank[gi + b][:, c:c + P], proj[:, t, o0:o0 + P], ident[:])
                        last.then_inc(p_qk, 1)
                    for pr in range(2):
                        for t in range(TT):
                            c = (2 * pr + t) * P
                            src = proj[:, t, ko + pr * P:ko + pr * P + P] if name != "C" else \
                                hn[:, t, 640 + pr * P:640 + pr * P + P]
                            last = nc.tensor.transpose(bank[4 + gi][:, c:c + P], src, ident[:])
                    last.then_inc(p_qk, 1)
                pe.wait_ge(a_q, 4 * l + 4)
                pe.wait_ge(v_keys, 3 * l + 3)
                n_units = PAIRS * TT
                for step in range(n_units + 2):
                    u = step
                    if u < n_units:
                        pr, t = u // 2, u % 2
                        if u >= 2:
                            pe.wait_ge(a_exp, n_units * l + u - 1)
                        nc.tensor.matmul(bank[u % 2][:, :], queries[:, pr, t * P:t * P + P],
                                         keys[:, KEYPAIR[pr]].rearrange("p h s -> p (h s)"),
                                         start=True, stop=True).then_inc(p_s, 1)
                    u = step - 1
                    if 0 <= u < n_units:
                        pe.wait_ge(a_exp, n_units * l + u + 1)
                        if u >= 2:
                            pe.wait_ge(a_pt, n_units * l + u - 1)
                        for c in range(4):
                            last = nc.tensor.transpose(bank[2 + u % 2][:, c * P:c * P + P],
                                                       prob[u % 2][:, c * P:c * P + P], ident[:])
                        last.then_inc(p_pt, 1)
                    u = step - 2
                    if u >= 0:
                        pe.wait_ge(a_pt, n_units * l + u + 1)
                        for h in range(2):
                            head, t = u // 2 * 2 + h, u % 2
                            if head < 8:
                                vcol = SEG["AB"[head // 4]][2] + head % 4 * HD
                            else:
                                vcol = SEG["C"][2] + (head - 8) // 4 * HD
                            for kt in range(TT):
                                last = nc.tensor.matmul(
                                    bank[4 + 2 * t + head // 8][:, head % 8 * HD:head % 8 * HD + HD],
                                    probT[u % 2][:, (2 * h + kt) * P:(2 * h + kt) * P + P],
                                    proj[:, kt, vcol:vcol + HD], start=(kt == 0), stop=(kt == 1))
                        last.then_inc(p_pv, 1)
                transposed_rows(l, 1)
                rows_ready(l, 1)
                pe.wait_ge(landed[3], 16 * (l * USES + 1))
                for n in range(4):
                    t, half = n // 2, n % 2
                    for k in range(KD):
                        last = nc.tensor.matmul(bank[4 + n][:, :], hT[:, k, t * P:t * P + P],
                                                slot8[3][:, k, half * 512:half * 512 + 512],
                                                start=(k == 0), stop=(k == KD - 1))
                    last.then_inc(p_out, 1)
                transposed_rows(l, 2)
                rows_ready(l, 2)
                pe.wait_ge(d_small, 80 * (l + 1))
                for t in range(TT):
                    for k in range(KD):
                        last = nc.tensor.matmul(bank[4][:, t * 36:t * 36 + 36], hT[:, k, t * P:t * P + P],
                                                w_route[:, k, :], start=(k == 0), stop=(k == KD - 1))
                last.then_inc(p_logit, 1)
                pe.wait_ge(v_chosen, l + 1)
                for c, terms in enumerate((((tri, 0),), ((tri, 1), (ones, 0)), ((ones, 0), (ones, 1)))):
                    for n, (w, t) in enumerate(terms):
                        last = nc.tensor.matmul(bank[5][:, c * NE:c * NE + NE], w[:], chosen[:, t, :],
                                                start=(n == 0), stop=(n == len(terms) - 1))
                last.then_inc(p_rank, 1)

            def gather(gq, pair=None, ps=None):
                pe.wait_ge(v_pick, gq + (AHEAD + 1))
                pe.wait_ge(v_xg, gq + AHEAD)
                pe.wait_ge(a_xg, gq + AHEAD)
                for k in range(KD):
                    n = 0
                    for t in range(TT):
                        for part in range(3):
                            last = nc.tensor.matmul(bank[k // 4][:, k % 4 * P:k % 4 * P + P], xpart[:, part, t, k, :],
                                                    pick[:, t, :], start=(n == 0), stop=(n == 5))
                            n += 1
                    if k % 4 == 3:
                        last.then_inc(p_gather, 1)

            def item(q, gq, slots, rounds, pair, has_next):
                def by_expert(b, weights, k_count, lhs, c0, s, done):
                    for k in range(k_count):
                        for e in range(2):
                            last = nc.tensor.matmul(bank[b][e * CAP:e * CAP + CAP, :], lhs[:, k, e * CAP:e * CAP + CAP],
                                                    weights[s][:, e, k, c0:c0 + 512],
                                                    start=(k == 0), stop=(k == k_count - 1))
                    last.then_inc(done, 1)

                pe.wait_ge(v_xg, gq + (AHEAD + 1))
                pe.wait_ge(a_xg, gq + (AHEAD + 1))
                pe.wait_ge(v_back[0], q + AHEAD)
                pe.wait_ge(landed[slots[0]], rounds[0] * 16 + 16)
                by_expert(2, slot_up, KD, xg, 0, slots[0], p_gate)
                pe.wait_ge(v_back[3], q + AHEAD)
                for t in range(TT):
                    last = nc.tensor.transpose(bank[5][:, t * P:t * P + P], pickw[:, t, :], ident[:])
                last.then_inc(p_pickT, 1)
                pe.wait_ge(v_back[1], q + AHEAD)
                pe.wait_ge(landed[slots[1]], rounds[1] * 16 + 16)
                by_expert(3, slot_up, KD, xg, 0, slots[1], p_up)
                if has_next:
                    gather(gq + 1)
                pe.wait_ge(v_hid, q + (AHEAD + 1))
                pe.wait_ge(v_back[2], q + AHEAD)
                hidc = hid.rearrange("p (f c) -> p c f", c=KE)
                for c in range(KE):
                    last = nc.tensor.transpose(bank[4][:, c * P:c * P + P], hidc[:, c, :], ident[:])
                last.then_inc(p_hidT, 1)
                pe.wait_ge(a_hidT, q + (AHEAD + 1))
                pe.wait_ge(landed[slots[2]], rounds[2] * 16 + 16)
                pe.wait_ge(a_y, q + AHEAD)
                by_expert(6, slot_dn, KE, hidT, 0, slots[2], p_down)
                pe.wait_ge(v_y, q + AHEAD)
                by_expert(7, slot_dn, KE, hidT, 512, slots[2], p_down)
                pe.wait_ge(a_pickT, q + (AHEAD + 1))
                pe.wait_ge(a_y, q + (AHEAD + 1))
                for n, (t, half) in enumerate(BACK):
                    if n == 2:
                        pe.wait_ge(v_y, q + (AHEAD + 1))
                    last = nc.tensor.matmul(bank[2 + n][:, :], pickT[:, t, :], y[:, half * 512:half * 512 + 512],
                                            start=True, stop=True)
                    last.then_inc(p_back, 1)

            run_layers(pe, extra, mixers, gather, item, seen[1])

        @block.scalar
        def _(act):
            extra = act.alloc_register("act_extra")
            act.reg_mov(extra, 0)
            for s in (a_silu, a_pickT, a_xg, a_hidT, a_y):
                act.sem_inc(s, AHEAD)
            n_units = PAIRS * TT

            def hT_odd_banks(l, n):
                for j in (1, 3):
                    act.wait_ge(p_tr, 12 * l + 4 * n + j + 1)
                    nc.scalar.copy(hT[:, 2 * j:2 * j + 2, :].rearrange("p k s -> p (k s)"), bank[j][:, :]).then_inc(a_hT, 1)

            def mean_squares(l, mark_value):
                act.wait_ge(v_x, mark_value)
                for t in range(TT):
                    last = nc.scalar.activation(hn[:, t, :], x[:, t, :], ACT.Square, scale=D ** -0.5,
                                                accum_out=ms[:, t:t + 1])
                last.then_inc(a_ss, 1)

            def mixers(l, e0):
                mean_squares(l, 2 * l + 1)
                hT_odd_banks(l, 0)
                act.wait_ge(d_skew, 16 * LAYERS)
                u = 0
                for s in range(3):
                    width = min(D, IN_COLS - s * D)
                    for c0 in range(0, width, 512):
                        w = min(512, width - c0)
                        for t in range(TT):
                            if u % 2:
                                act.wait_ge(p_proj, 10 * l + u + 1)
                                nc.scalar.copy(proj[:, t, s * D + c0:s * D + c0 + w], bank[4 + u % 4][:, 0:w]).then_inc(a_proj, 1)
                            u += 1
                act.wait_ge(v_proj, 5 * l + 5)
                act.wait_ge(a_proj, 5 * l + 5)
                for gi, name in enumerate(GROUPS):
                    qo, _, vo, _, _ = SEG[name]
                    if name == "C":
                        act.wait_ge(v_ssh, 6 * l + 4)
                    for t in range(TT):
                        dst = hn[:, t, 512:1024] if name == "B" else hn[:, t, 0:vo - qo]
                        nc.scalar.activation(dst, proj[:, t, qo:vo], ACT.Square, scale=HD ** -0.5).then_inc(a_sq, 1)
                for b, n in enumerate((1, 3, 5, 6)):
                    act.wait_ge(p_qk, 7 * l + n)
                    nc.scalar.copy(queries[:, 2 * b:2 * b + 2, :].rearrange("p k s -> p (k s)"), bank[b][:, :]).then_inc(a_q, 1)
                for step in range(n_units + 1):
                    u = step
                    if u < n_units:
                        act.wait_ge(v_soft, n_units * l + u + 1)
                        if u >= 2:
                            act.wait_ge(p_pt, n_units * l + u - 1)
                        pr, t = u // 2, u % 2
                        for h in range(2):
                            dst = prob[u % 2][:, h * SEQ:h * SEQ + SEQ]
                            src = dst if pr < 4 else bank[u % 2][:, h * SEQ:h * SEQ + SEQ]
                            last = nc.scalar.activation(dst, src, ACT.Exp, bias=nmax[:, u % 2, h:h + 1],
                                                        scale=1.0 if pr < 4 else SCALE,
                                                        accum_out=den[:, t, 2 * pr + h:2 * pr + h + 1])
                        last.then_inc(a_exp, 1)
                    u = step - 1
                    if u >= 0:
                        act.wait_ge(p_pt, n_units * l + u + 1)
                        if u >= 2:
                            act.wait_ge(p_pv, n_units * l + u - 1)
                        nc.scalar.copy(probT[u % 2], bank[2 + u % 2][:, :]).then_inc(a_pt, 1)
                act.wait_ge(v_o, 4 * l + 4)
                for t in range(TT):
                    for n, (c0, w) in enumerate(((0, 256), (256, 256), (512, 512))):
                        last = nc.scalar.activation(work[:, t * D + c0:t * D + c0 + w], hn[:, t, c0:c0 + w], ACT.Square,
                                                    scale=w ** -0.5, accum_out=ms[:, 3 * t + n:3 * t + n + 1])
                last.then_inc(a_ss, 1)
                hT_odd_banks(l, 1)
                mean_squares(l, 2 * l + 2)
                hT_odd_banks(l, 2)
                act.wait_ge(v_hn, 6 * l + 6)
                for t in range(TT):
                    last = nc.scalar.copy(xpart[:, 0, t], hn_kc[:, t])
                last.then_inc(a_part, 1)
                act.wait_ge(v_router, 2 * l + 1)
                nc.scalar.activation(rb[:, :, 0:NG], ra[:, :, 0:NG], ACT.Exp).then_inc(a_rexp, 1)
                act.wait_ge(v_router, 2 * l + 2)
                nc.scalar.activation(col[:, 4, :], col[:, 3, :], ACT.Exp).then_inc(a_rexp, 1)
                act.wait_ge(v_part, 2 * l + 1)
                for t in range(TT):
                    last = nc.scalar.copy(xpart[:, 1, t], hn_kc[:, t])
                last.then_inc(a_part, 1)

            def gathered(gq, pair=None, ps=None):
                act.wait_ge(p_gather, gq * 2 + (AHEAD + 2))
                nc.scalar.copy(xg[:, 4:8, :].rearrange("p k s -> p (k s)"), bank[1][:, :]).then_inc(a_xg, 1)

            def item(q, gq, slots, rounds, pair, has_next):
                act.wait_ge(p_pickT, q + (AHEAD + 1))
                act.wait_ge(p_back, q * 4 + AHEAD)
                nc.scalar.copy(pickT.rearrange("p t s -> p (t s)"), bank[5][:, 0:2 * P]).then_inc(a_pickT, 1)
                act.wait_ge(p_gate, q + (AHEAD + 1))
                act.wait_ge(p_hidT, q + AHEAD)
                nc.scalar.activation(hid, bank[2][:, :], ACT.Silu).then_inc(a_silu, 1)
                if has_next:
                    act.wait_ge(p_up, q + (AHEAD + 1))
                    gathered(gq + 1)
                act.wait_ge(p_hidT, q + (AHEAD + 1))
                act.wait_ge(p_down, q * 2 + AHEAD)
                nc.scalar.copy(hidT.rearrange("p c s -> p (c s)"), bank[4][:, :]).then_inc(a_hidT, 1)
                act.wait_ge(p_down, q * 2 + (AHEAD + 1))
                nc.scalar.copy(y[:, 0:512], bank[6][:, :]).then_inc(a_y, 1)

            run_layers(act, extra, mixers, gathered, item, seen[2])

        @block.vector
        def _(dve):
            extra = dve.alloc_register("dve_extra")
            dve.reg_mov(extra, 0)
            for s in (v_pick, v_xg, v_hid, v_y, v_istep, *v_back):
                dve.sem_inc(s, AHEAD)
            n_units = PAIRS * TT
            steps = [0, 0]
            tt, ts, stt = nc.vector.tensor_tensor, nc.vector.tensor_scalar, nc.vector.scalar_tensor_tensor

            def link(ins):
                steps[0] += 1
                ins.then_inc(v_step, 1)
                dve.wait_ge(v_step, steps[1] * V_STEPS + steps[0])

            def wide(ap, n):
                return ap.unsqueeze(len(ap.shape)).broadcast_to(list(ap.shape) + [n])

            def over(ap, axis, n):
                shape = list(ap.shape)
                shape.insert(axis, n)
                return ap.unsqueeze(axis).broadcast_to(shape)

            def hT_even_banks(l, n):
                for j in (0, 2):
                    dve.wait_ge(p_tr, 12 * l + 4 * n + j + 1)
                    nc.vector.tensor_copy(hT[:, 2 * j:2 * j + 2, :].rearrange("p k s -> p (k s)"), bank[j][:, :]).then_inc(v_hT, 1)

            def norm_rows(l, rstd_value, gain_value):
                dve.wait_ge(g_rstd, 4 * l + rstd_value)
                dve.wait_ge(d_gain, 48 * l + 16 * gain_value)
                for t in range(TT):
                    stt(hn[:, t, :], x[:, t, :], rstd[:, t:t + 1], gain[:], ALU.mult, ALU.mult).then_inc(v_hn, 1)

            def mixers(l, e0):
                steps[0], steps[1] = 0, l
                dve.wait_ge(d_x, 16)
                dve.wait_ge(d_const, 16 * 8)
                for n in range(4):
                    dve.wait_ge(v_back[n], l * EPAIRS + e0 + AHEAD)
                nc.vector.memset(mark[:], 0.0).then_inc(v_x, 1)
                norm_rows(l, 1, 1)
                hT_even_banks(l, 0)
                dve.wait_ge(d_rel, 64 * (l + 1))
                rel28 = rel[:].rearrange("p h r c -> p (h r) c")
                link(tt(rel28, rel28, over(colmask[:], 1, 28), ALU.add))
                dve.wait_ge(d_skew, 16 * LAYERS)
                u = 0
                for s in range(3):
                    width = min(D, IN_COLS - s * D)
                    for c0 in range(0, width, 512):
                        w = min(512, width - c0)
                        for t in range(TT):
                            if u % 2 == 0:
                                dve.wait_ge(p_proj, 10 * l + u + 1)
                                nc.vector.tensor_copy(proj[:, t, s * D + c0:s * D + c0 + w], bank[4 + u % 4][:, 0:w]).then_inc(v_proj, 1)
                            u += 1
                n = 0
                for name in GROUPS:
                    qo, _, vo, nq, nk = SEG[name]
                    h0 = HEAD0[name]
                    for t in range(TT):
                        dve.wait_ge(a_sq, 6 * l + n + 1)
                        src = hn[:, t, 512:1024] if name == "B" else hn[:, t, 0:vo - qo]
                        nc.vector.tensor_reduce(msh[:, t, h0:h0 + nq + nk], src.rearrange("p (h d) -> p h d", d=HD),
                                                AX_X, ALU.add).then_inc(v_ssh, 1)
                        n += 1
                dve.wait_ge(a_proj, 5 * l + 5)
                dve.wait_ge(v_proj, 5 * l + 5)
                dve.wait_ge(g_rstd, 4 * l + 2)
                dve.wait_ge(d_small, 80 * (l + 1))
                for gi, name in enumerate(GROUPS):
                    qo, ko, vo, nq, nk = SEG[name]
                    h0 = HEAD0[name]
                    heads = proj[:, :, qo:vo].rearrange("p t (h d) -> p t h d", d=HD)
                    link(tt(heads, heads, wide(rsh[:, :, h0:h0 + nq + nk], HD), ALU.mult))
                    qh, kh = heads[:, :, 0:nq, :], heads[:, :, nq:, :]
                    gq = over(over(qkg[:, 2 * gi, :], 1, nq), 1, TT)
                    gk = over(over(qkg[:, 2 * gi + 1, :], 1, nk), 1, TT)
                    if name != "C":
                        tt(qh, qh, gq, ALU.mult)
                        tt(kh, kh, gk, ALU.mult).then_inc(v_qk, 1)
                        continue
                    tt(qh, qh, gq, ALU.mult)
                    link(tt(kh, kh, gk, ALU.mult))
                    part = hn[:, :, 0:(nq + nk) * HD].rearrange("p t (h d) -> p t h d", d=HD)
                    for t in range(TT):
                        src = heads[:, t].rearrange("p h (a b f) -> p h a b f", a=2, b=2)
                        dst = part[:, t].rearrange("p h (a b f) -> p h a b f", a=2, b=2)
                        sin = rope[:, t, 1, :].rearrange("p (a b f) -> p a b f", a=2, b=2)
                        for b in range(2):
                            last = tt(dst[:, :, :, b, :], src[:, :, :, 1 - b, :], over(sin[:, :, b, :], 1, nq + nk), ALU.mult)
                    link(last)
                    for t in range(TT):
                        last = tt(heads[:, t], heads[:, t], over(rope[:, t, 0, :], 1, nq + nk), ALU.mult)
                    link(last)
                    for t in range(TT):
                        tt(hn[:, t, 640:896].rearrange("p (k c d) -> p k c d", k=nk, c=2),
                           over(heads[:, t, nq:, :], 2, 2), over(part[:, t, nq:, :], 2, 2), ALU.add)
                    tt(qh, qh, part[:, :, 0:nq, :], ALU.add).then_inc(v_qk, 1)
                dve.wait_ge(g_keys0, l + 1)
                for gi in range(3):
                    dve.wait_ge(p_qk, 7 * l + (2, 4, 7)[gi])
                    for h in range(2):
                        src = bank[4 + gi][64 * h:64 * h + 64, :].rearrange("p (j s) -> p j s", j=2)
                        last = nc.vector.tensor_copy(keys[64 * h:64 * h + 64, 2 * gi:2 * gi + 2, h, :], src)
                    last.then_inc(v_keys, 1)
                for u in range(n_units):
                    pr, t = u // 2, u % 2
                    dve.wait_ge(p_s, n_units * l + u + 1)
                    if u >= 2:
                        dve.wait_ge(p_pt, n_units * l + u - 1)
                    sc = bank[u % 2][:, :].rearrange("p (h s) -> p h s", h=2)
                    pb = prob[u % 2].rearrange("p (h s) -> p h s", h=2)
                    if pr < 2:
                        for rr in range(2):
                            r = 2 * t + rr
                            rows = slice(64 * rr, 64 * rr + 64)
                            last = stt(pb[rows], sc[rows], SCALE,
                                       rel[rows, 2 * pr:2 * pr + 2, 3 - r:7 - r, :].rearrange("p h r c -> p h (r c)"),
                                       ALU.mult, ALU.add)
                        link(last)
                        nc.vector.tensor_reduce(nmax[:, u % 2, 0:2], pb, AX_X, ALU.max, negate=True).then_inc(v_soft, 1)
                    elif pr < 4:
                        c0 = (1 - t) * P
                        link(stt(pb, sc, SCALE, dil[:, 2 * pr - 4:2 * pr - 2, c0:c0 + SEQ], ALU.mult, ALU.add))
                        nc.vector.tensor_reduce(nmax[:, u % 2, 0:2], pb, AX_X, ALU.max, negate=True).then_inc(v_soft, 1)
                    else:
                        link(nc.vector.tensor_reduce(nmax[:, u % 2, 2:4], sc, AX_X, ALU.max, negate=True))
                        ts(nmax[:, u % 2, 0:2], nmax[:, u % 2, 2:4], SCALE, None, ALU.mult).then_inc(v_soft, 1)
                dve.wait_ge(a_exp, n_units * (l + 1))
                link(nc.vector.reciprocal(rden[:], den[:]))
                dve.wait_ge(p_pv, n_units * (l + 1))
                for t in range(TT):
                    for b in range(2):
                        tt(hn[:, t, b * 512:b * 512 + 512].rearrange("p (h d) -> p h d", d=HD),
                           bank[4 + 2 * t + b][:, :].rearrange("p (h d) -> p h d", d=HD),
                           wide(rden[:, t, 8 * b:8 * b + 8], HD), ALU.mult).then_inc(v_o, 1)
                dve.wait_ge(v_o, 4 * l + 4)
                dve.wait_ge(g_rstd, 4 * l + 3)
                dve.wait_ge(d_gain, 48 * l + 32)
                for t in range(TT):
                    for n, (c0, w) in enumerate(((0, 256), (256, 256), (512, 512))):
                        last = stt(hn[:, t, c0:c0 + w], hn[:, t, c0:c0 + w], rstd[:, 3 * t + n:3 * t + n + 1],
                                   gain[:, c0:c0 + w], ALU.mult, ALU.mult)
                    last.then_inc(v_hn, 1)
                hT_even_banks(l, 1)
                for n in range(4):
                    t, half = n // 2, n % 2
                    dve.wait_ge(p_out, 4 * l + n + 1)
                    xs = x[:, t, half * 512:half * 512 + 512]
                    last = tt(xs, xs, bank[4 + n][:, :], ALU.add)
                last.then_inc(v_x, 1)
                dve.wait_ge(v_x, 2 * l + 2)
                norm_rows(l, 4, 3)
                hT_even_banks(l, 2)
                dve.wait_ge(a_part, 2 * l + 1)
                dve.wait_ge(p_tr, 12 * l + 12)
                for t in range(TT):
                    last = tt(hn_kc[:, t], hn_kc[:, t], xpart[:, 0, t], ALU.subtract)
                last.then_inc(v_part, 1)
                dve.wait_ge(p_logit, l + 1)
                dve.wait_ge(d_small, 80 * (l + 1))
                link(tt(lg[:], bank[4][:, 0:72].rearrange("p (t n) -> p t n", t=TT), over(b_route[:], 1, TT), ALU.add))
                gl, el = lg[:, :, 0:NG], lg[:, :, NG:36]
                link(nc.vector.tensor_reduce(col[:, 0, :], gl, AX_X, ALU.max))
                tt(ra[:, :, 0:NG], gl, wide(col[:, 0, :], NG), ALU.subtract).then_inc(v_router, 1)
                dve.wait_ge(v_router, 2 * l + 1)

                def first_of_max(dst, score, diff, n, r0, c):
                    link(stt(score, diff, 0.0, over(rev[:, r0:r0 + n], 1, TT), ALU.is_equal, ALU.mult))
                    link(nc.vector.tensor_reduce(col[:, c, :], score, AX_X, ALU.max))
                    link(tt(dst, score, wide(col[:, c, :], n), ALU.is_equal))

                first_of_max(ra[:, :, 8:12], ra[:, :, 4:8], ra[:, :, 0:NG], NG, 0, 1)
                link(ts(ra[:, :, 12:16], ra[:, :, 8:12], BIG, -BIG, ALU.mult, ALU.add))
                link(tt(el.rearrange("p t (g e) -> p t g e", g=NG), el.rearrange("p t (g e) -> p t g e", g=NG),
                        wide(ra[:, :, 12:16], EPG), ALU.add))
                link(nc.vector.tensor_reduce(col[:, 1, :], el, AX_X, ALU.max))
                dve.wait_ge(a_rexp, 2 * l + 1)
                link(nc.vector.tensor_reduce(col[:, 5, :], rb[:, :, 0:NG], AX_X, ALU.add))
                link(tt(ra[:, :, 4:36], el, wide(col[:, 1, :], NE), ALU.subtract))
                first_of_max(oh1[:], rb[:, :, 4:36], ra[:, :, 4:36], NE, 4, 6)
                link(stt(el, oh1[:], -BIG, el, ALU.mult, ALU.add))
                link(nc.vector.tensor_reduce(col[:, 2, :], el, AX_X, ALU.max))
                tt(col[:, 3, :], col[:, 2, :], col[:, 1, :], ALU.subtract).then_inc(v_router, 1)
                link(tt(ra[:, :, 4:36], el, wide(col[:, 2, :], NE), ALU.subtract))
                first_of_max(oh2[:], rb[:, :, 4:36], ra[:, :, 4:36], NE, 4, 6)
                tt(chosen[:], oh1[:], oh2[:], ALU.add).then_inc(v_chosen, 1)
                link(nc.vector.reciprocal(col[:, 7, :], col[:, 5, :]))
                dve.wait_ge(a_rexp, 2 * l + 2)
                link(ts(col[:, 8, :], col[:, 4, :], 1.0, None, ALU.add))
                link(nc.vector.reciprocal(col[:, 9, :], col[:, 8, :]))
                link(tt(col[:, 10, :], col[:, 9, :], col[:, 7, :], ALU.mult))
                link(tt(col[:, 11, :], col[:, 10, :], col[:, 4, :], ALU.mult))
                tt(oh1[:], oh1[:], wide(col[:, 10, :], NE), ALU.mult)
                link(tt(oh2[:], oh2[:], wide(col[:, 11, :], NE), ALU.mult))
                tt(rg[:, TT:2 * TT, 0:NE], oh1[:], oh2[:], ALU.add)
                nc.vector.memset(rg[:, :, NE:], -1.0)
                dve.wait_ge(p_rank, l + 1)
                dve.wait_ge(v_chosen, l + 1)
                link(stt(rb[:, :, 0:NE], bank[5][:, 0:2 * NE].rearrange("p (t n) -> p t n", t=TT), 1.0, chosen[:],
                         ALU.add, ALU.mult))
                link(ts(rg[:, 0:TT, 0:NE], rb[:, :, 0:NE], -1.0, None, ALU.add))
                counts = bank[5][0:1, 2 * NE:3 * NE].rearrange("p (j e) -> p j e", e=2)
                link(nc.vector.tensor_reduce(pairmax[:], counts, AX_X, ALU.max))
                for ps in range(PASSES - 1):
                    last = ts(flags[0:1, ps * EPAIRS:ps * EPAIRS + EPAIRS], pairmax[:], float(CAP * (ps + 1)), None, ALU.is_gt)
                link(last)
                nc.vector.tensor_reduce(flags[0:1, (PASSES - 1) * EPAIRS:(PASSES - 1) * EPAIRS + 1],
                                        flags[0:1, 0:EPAIRS], AX_X, ALU.max).then_inc(v_flags, 1)
                dve.wait_ge(a_part, 2 * l + 2)
                for t in range(TT):
                    last = tt(xpart[:, 2, t], hn_kc[:, t], xpart[:, 1, t], ALU.subtract)
                last.then_inc(v_part, 1)
                assert steps[0] == V_STEPS, steps

            def picks(gq, pair, ps):
                nc.vector.tensor_copy(rgc[:], rg[:, :, bass.ds(pair * 2, 2)] if not isinstance(pair, int)
                                      else rg[:, :, 2 * pair:2 * pair + 2]).then_inc(v_istep, 1)
                dve.wait_ge(v_istep, gq * 2 + (AHEAD + 1))
                places = iota[:, 0:CAP] if ps is None else iota[:, bass.ds(ps * CAP + CAP, CAP)]
                hot = pick.rearrange("p t (e s) -> p (t e) s", e=2)
                tt(hot, over(places, 1, 2 * TT), wide(rgc[:, 0:TT, :].rearrange("p t e -> p (t e)"), CAP),
                   ALU.is_equal).then_inc(v_istep, 1)
                dve.wait_ge(v_istep, gq * 2 + (AHEAD + 2))
                tt(pickw.rearrange("p t (e s) -> p (t e) s", e=2), hot,
                   wide(rgc[:, TT:2 * TT, :].rearrange("p t e -> p (t e)"), CAP), ALU.mult).then_inc(v_pick, 1)

            def copy_gathered(gq):
                dve.wait_ge(p_gather, gq * 2 + (AHEAD + 1))
                nc.vector.tensor_copy(xg[:, 0:4, :].rearrange("p k s -> p (k s)"), bank[0][:, :]).then_inc(v_xg, 1)

            def first(gq, pair, ps):
                picks(gq, pair, ps)
                copy_gathered(gq)

            def item(q, gq, slots, rounds, pair, has_next):
                if has_next:
                    dve.wait_ge(p_pickT, q + (AHEAD + 1))
                    picks(gq + 1, pair + 1, None)
                dve.wait_ge(a_silu, q + (AHEAD + 1))
                dve.wait_ge(p_up, q + (AHEAD + 1))
                tt(hid, hid, bank[3][:, :], ALU.mult).then_inc(v_hid, 1)
                if has_next:
                    copy_gathered(gq + 1)
                dve.wait_ge(p_down, q * 2 + (AHEAD + 2))
                dve.wait_ge(p_back, q * 4 + AHEAD)
                nc.vector.tensor_copy(y[:, 512:1024], bank[7][:, :]).then_inc(v_y, 1)
                for n, (t, half) in enumerate(BACK):
                    dve.wait_ge(p_back, q * 4 + (AHEAD + n + 1))
                    dve.wait_ge(v_back[n], q + AHEAD)
                    xs = x[:, t, half * 512:half * 512 + 512]
                    tt(xs, xs, bank[2 + n][:, :], ALU.add).then_inc(v_back[n], 1)

            run_layers(dve, extra, mixers, first, item, seen[3])
            e = dve.snap(extra, min_val=0, max_val=96)
            for n in range(4):
                dve.wait_ge(v_back[n], e + (LAYERS * EPAIRS + AHEAD))
            nc.vector.memset(mark[:], 0.0).then_inc(v_x, 1)


_INS = ["x", "norm1_g", "w_in", "qk_norm_g", "na_rpb", "mix_norm_g", "w_out", "norm2_g", "w_router_group",
        "b_router_group", "w_router_expert", "b_router_expert", "w_gate", "w_up", "w_down"]


def shape_constants():
    t = np.arange(SEQ)
    nf = HD // 4
    inv = (10000.0 ** (-np.arange(nf, dtype=np.float32) / nf)).astype(np.float32)
    ang = np.stack([(t // GRID).astype(np.float32)[:, None] * inv, (t % GRID).astype(np.float32)[:, None] * inv], 1)
    cos = np.repeat(np.cos(ang)[:, :, None, :], 2, axis=2).reshape(SEQ, HD)
    sin = np.stack([-np.sin(ang), np.sin(ang)], axis=2).reshape(SEQ, HD)
    rope = np.stack([cos, sin], 1).reshape(TT, P, 2, HD).transpose(1, 0, 2, 3)
    c = np.arange(P)[:, None] % GRID
    start = np.clip(c - 8, 0, GRID - 16)
    kc = np.arange(GRID)[None, :]
    colmask = np.where((kc >= start) & (kc < start + 16), 0.0, -BIG)
    dist = np.abs(np.arange(P)[:, None] - (np.arange(3 * P)[None, :] - P))
    count = (dist <= 64).astype(int) + ((dist % 4 == 0) & (dist <= 256)) + ((dist % 16 == 0) & (dist <= 1024))
    slope = 2.0 ** (-8.0 * np.arange(1, 5) / 4)
    base = np.where(count > 0, np.log(np.maximum(count, 1)), -BIG)
    dil = base[:, None, :] - slope[None, :, None] * dist[:, None, :] * (count > 0)[:, None, :]
    return {
        "c_rope": np.ascontiguousarray(rope, np.float32), "c_colmask": colmask.astype(np.float32),
        "c_ident": np.eye(P, dtype=np.float32), "c_dil": dil.astype(np.float32),
        "c_tri": np.triu(np.ones((P, P)), 1), "c_ones": np.ones((P, P)),
        "c_iota": np.tile(np.arange(SEQ, dtype=np.float32), (P, 1)),
        "c_rev": np.tile(np.concatenate([np.arange(4, 0, -1), np.arange(32, 0, -1)]).astype(np.float32), (P, 1)),
    }


def kernel(**inputs):
    import ml_dtypes
    import concourse.bacc as _bacc
    from concourse import mybir as _mybir
    from concourse.bass_utils import run_bass_kernel_spmd as _run

    nc = _bacc.Bacc("TRN2", target_bir_lowering=False, num_devices=1)
    arrays, aps = {}, {}
    consts = shape_constants()
    for name in ("c_tri", "c_ones"):
        consts[name] = consts[name].astype(ml_dtypes.bfloat16)
    for name, value in list({n: inputs[n] for n in _INS}.items()) + list(consts.items()):
        v = np.ascontiguousarray(value)
        arrays[f"in_{name}"] = v
        aps[name] = nc.dram_tensor(f"in_{name}", v.shape, _mybir.dt.from_np(v.dtype), kind="ExternalInput").ap()
    out = nc.dram_tensor("out", (1, SEQ, D), _mybir.dt.float32, kind="ExternalOutput").ap()
    encoder(nc, aps, out)
    r = _run(nc, [arrays], core_ids=[0])
    return r.results[0]["out"]
```

```python
from contextlib import ExitStack

import numpy as np

import concourse.bass as bass
from concourse import mybir

F32 = mybir.dt.float32
BF16 = mybir.dt.bfloat16
I32 = mybir.dt.int32
ALU = mybir.AluOpType
ACT = mybir.ActivationFunctionType
AX_X = mybir.AxisListType.X

P = 128
LAYERS = 2
SEQ, D = 256, 1024
TT = SEQ // P
KD = D // P
HD = 64
IN_COLS = 2304
EPS = 1e-6
BIG = 1e30
GRID = 64
SCALE = HD ** -0.5

SEG = {"A": (0, 256, 512, 4, 4), "B": (768, 1024, 1280, 4, 4), "C": (1536, 2048, 2176, 8, 2)}
HEAD0 = {"A": 0, "B": 8, "C": 16}
NHEAD = 26
GROUPS = ("C", "A", "B")
SEG_COLS = 768
HALF_SEG = SEG_COLS // 2
PAIRS = 8
ORDER = (4, 5, 6, 7, 0, 1, 2, 3)
N_UNITS = PAIRS * TT
KEYPAIR = [0, 1, 2, 3, 4, 4, 5, 5]

NG, NE, EPG = 4, 32, 8
DE = 512
KE = DE // P
CAP = 64
EPAIRS = NE // 2
PASSES = SEQ // CAP
AGAIN = 8
UNROLL = 4
AHEAD = 3
SLOT = 8192
SLOTS = 4
MIX_USES = 1
MOE_USES = 3 * EPAIRS // SLOTS
USES = MIX_USES + MOE_USES

PROJ = TT * IN_COLS
KEYS = 6 * 2 * SEQ
WORK = PROJ + KEYS


def encoder(nc, a, out):
    ctx = ExitStack()
    with ctx:
        def sb(name, shape, dt=F32):
            return ctx.enter_context(nc.sbuf_tensor(name, shape, dt))

        def sem(name):
            return ctx.enter_context(nc.semaphore(name))

        ring = [sb(f"ring{i}", [P, SLOT]) for i in range(SLOTS)]
        x = sb("x", [P, TT, D])
        hn = sb("hn", [P, TT, D])
        hT = sb("hT", [P, KD, SEQ])
        work = sb("work", [P, WORK])
        rel = sb("rel", [P, 4, 7, GRID])
        dil = sb("dil", [P, 4, 3 * P])
        gain = sb("gain", [P, D])
        qkg = sb("qkg", [P, 6, HD])
        rope = sb("rope", [P, TT, 2, HD])
        colmask = sb("colmask", [P, GRID])
        ident = sb("ident", [P, P])
        tri = sb("tri", [P, P], BF16)
        ones = sb("ones", [P, P], BF16)
        iota = sb("iota", [P, SEQ])
        rev = sb("rev", [P, 36])
        w_route = sb("w_route", [P, KD, 36])
        b_route = sb("b_route", [P, 36])
        ms = sb("ms", [P, 8])
        rstd = sb("rstd", [P, 8])
        msh = sb("msh", [P, TT, NHEAD])
        rsh = sb("rsh", [P, TT, NHEAD])
        mhalf = sb("mhalf", [P, 1])
        eps = sb("eps", [P, 1])
        nmax = sb("nmax", [P, 2, 4])
        den = sb("den", [P, TT, 16])
        rden = sb("rden", [P, TT, 16])
        col = sb("col", [P, 12, TT])
        rg = sb("rg", [P, 2 * TT, NE + 2])
        rgc = sb("rgc", [P, 2 * TT, 2])
        again = sb("again", [1, 2 * AGAIN + 1], I32)
        pairmax = sb("pairmax", [1, EPAIRS])
        mark = sb("mark", [1, 8])

        proj = work[:, 0:PROJ].rearrange("p (t c) -> p t c", t=TT)
        keys = work[:, PROJ:WORK].rearrange("p (j h s) -> p j h s", j=6, h=2)
        prob = [work[:, c:c + 512] for c in (0, IN_COLS)]
        probT = [work[:, c + SEG["C"][0]:c + SEG["C"][0] + 512] for c in (0, IN_COLS)]
        o = [0]

        def carve(n):
            o[0] += n
            return work[:, o[0] - n:o[0]]

        xpart = carve(3 * TT * D // 2).bitcast(BF16).rearrange("p (i t k c) -> p i t k c", i=3, t=TT, k=KD)
        pick = carve(TT * P // 2).bitcast(BF16).rearrange("p (t s) -> p t s", t=TT)
        pickw = carve(TT * P).rearrange("p (t s) -> p t s", t=TT)
        pickT = carve(TT * P).rearrange("p (t s) -> p t s", t=TT)
        xg = carve(KD * P).rearrange("p (k s) -> p k s", k=KD)
        hid = carve(DE)
        hidT = carve(DE).rearrange("p (c s) -> p c s", c=KE)
        y = carve(D)
        lg, ra, rb = (carve(TT * 36).rearrange("p (t n) -> p t n", t=TT) for _ in range(3))
        oh1, oh2 = (carve(TT * NE).rearrange("p (t n) -> p t n", t=TT) for _ in range(2))
        chosen = carve(TT * NE // 2).bitcast(BF16).rearrange("p (t n) -> p t n", t=TT)
        hT_flat = hT[:].rearrange("p k s -> p (k s)")
        flip = hT_flat[0:GRID, 0:P]
        relrev = hT_flat[0:GRID, P:P + 28 * GRID].rearrange("p (h r c) -> p h r c", h=4, r=7)

        bank = [ctx.enter_context(nc.psum_tensor(f"bank{i}", [P, 512], F32)) for i in range(8)]

        d_x, d_first, d_const, d_rel = sem("d_x"), sem("d_first"), sem("d_const"), sem("d_rel")
        d_gain1, d_gain, d_small, d_out = sem("d_gain1"), sem("d_gain"), sem("d_small"), sem("d_out")
        landed = [sem(f"landed{i}") for i in range(SLOTS)]
        p_tr, p_proj, p_qk, p_s, p_pt, p_pv = (sem("p_" + n) for n in ("tr", "proj", "qk", "s", "pt", "pv"))
        p_out, p_logit, p_rank, p_flip = sem("p_out"), sem("p_logit"), sem("p_rank"), sem("p_flip")
        p_gather, p_gate, p_up, p_pickT, p_hidT, p_down, p_back = (
            sem("p_" + n) for n in ("gather", "gate", "up", "pickT", "hidT", "down", "back"))
        a_ss, a_hT, a_proj, a_sq, a_q, a_exp, a_pt = (sem("a_" + n) for n in ("ss", "hT", "proj", "sq", "q", "exp", "pt"))
        a_rexp, a_part, a_silu, a_pickT, a_xg, a_hidT, a_y = (
            sem("a_" + n) for n in ("rexp", "part", "silu", "pickT", "xg", "hidT", "y"))
        v_x, v_hn, v_hT, v_proj, v_ssh, v_qk, v_keys, v_soft = (
            sem("v_" + n) for n in ("x", "hn", "hT", "proj", "ssh", "qk", "keys", "soft"))
        v_rel = sem("v_rel")
        v_o, v_router, v_chosen, v_flags, v_res, v_part, v_step = (
            sem("v_" + n) for n in ("o", "router", "chosen", "flags", "res", "part", "step"))
        v_pick, v_xg, v_hid, v_y, v_istep = (sem("v_" + n) for n in ("pick", "xg", "hid", "y", "istep"))
        v_back = [sem(f"v_back{n}") for n in range(4)]
        g_init, g_rstd, g_step, g_keys0 = sem("g_init"), sem("g_rstd"), sem("g_step"), sem("g_keys0")
        seen = [sem(f"seen{i}") for i in range(5)]

        slot8 = [r[:, :].rearrange("p (k c) -> p k c", k=KD) for r in ring]
        slot_up = [r[:, :].rearrange("p (e k c) -> p e k c", e=2, k=KD) for r in ring]
        slot_dn = [r[:, :].rearrange("p (e k c) -> p e k c", e=2, k=KE) for r in ring]
        V_STEPS = 58

        def slot_of(i, j):
            u = 3 * i + j
            return u % SLOTS, u // SLOTS

        def run_layers(eng, extra, mixers, first, item, seen_sem):
            with eng.Fori(0, LAYERS) as l:
                e0 = eng.snap(extra, min_val=0, max_val=96)
                mixers(l, e0)
                first(eng.snap(l * (EPAIRS + 1) + e0, min_val=0, max_val=1000), 0, None)
                with eng.Fori(0, EPAIRS // UNROLL) as i4:
                    for ii in range(UNROLL):
                        q = eng.snap(l * EPAIRS + e0 + i4 * UNROLL + ii, min_val=0, max_val=1000)
                        so = [slot_of(ii, j) for j in range(3)]
                        rounds = [i4 * 3 + l * USES + (MIX_USES + r) + (e0 if s < 3 else 0) for s, r in so]
                        item(q, q + l, [s for s, _ in so], rounds, i4 * UNROLL + ii, True)
                eng.wait_ge(v_flags, l + 1)
                eng.sem_inc(seen_sem, 1)
                count = eng.value_load(again[0:1, 2 * AGAIN:2 * AGAIN + 1], min_val=0, max_val=AGAIN)
                with eng.If(count):
                    with eng.Fori(0, count) as j:
                        pair = eng.value_load(again[0:1, bass.ds(j, 1)], min_val=0, max_val=EPAIRS - 1)
                        ps = eng.value_load(again[0:1, bass.ds(j + AGAIN, 1)], min_val=0, max_val=PASSES - 2)
                        e = eng.snap(extra, min_val=0, max_val=96)
                        q = eng.snap(l * EPAIRS + EPAIRS + e, min_val=0, max_val=1000)
                        gq = eng.snap(q + l + 1, min_val=0, max_val=1000)
                        first(gq, pair, ps)
                        item(q, gq, [0, 1, 2], [l * USES + USES + e] * 3, pair, False)
                        eng.reg_add(extra, extra, 1)

        block = ctx.enter_context(nc.Block())

        @block.sync
        def _(sp):
            extra = sp.alloc_register("sp_extra")
            sp.reg_mov(extra, 0)
            xr = a["x"].rearrange("b (t p) d -> (b p) t d", t=TT)
            sp.dma_start(x[:, :, :], xr).then_inc(d_x, 16)
            for name, dst in (("c_ident", ident), ("c_colmask", colmask)):
                sp.dma_start(dst[:], a[name]).then_inc(d_first, 16)

            def spread(src):
                return src.partition_broadcast(P).rearrange("p a c -> p (a c)")

            def small_loads(l):
                sp.dma_start(qkg[:], a["qk_norm_g"][bass.ds(l, 1)].rearrange("l m q d -> l (m q) d").partition_broadcast(P)
                             .rearrange("p l m d -> p (l m) d")).then_inc(d_small, 16)
                for w_name, b_name, lo, hi in (("w_router_group", "b_router_group", 0, NG),
                                               ("w_router_expert", "b_router_expert", NG, 36)):
                    sp.dma_start(w_route[:, :, lo:hi], a[w_name][bass.ds(l, 1)].rearrange("l (p k) n -> (l p) k n", k=KD)).then_inc(d_small, 16)
                    sp.dma_start(b_route[:, lo:hi], spread(a[b_name][bass.ds(l, 1), :])).then_inc(d_small, 16)

            def load_pair(pair, l, slots, free):
                for j, name in enumerate(("w_gate", "w_up", "w_down")):
                    s = slots[j]
                    free[j]()
                    k = KE if name == "w_down" else KD
                    src = a[name][bass.ds(l, 1), bass.ds(pair, 2)].rearrange("l e (p k) c -> p (l e) k c", k=k)
                    sp.dma_start(slot_dn[s] if name == "w_down" else slot_up[s], src).then_inc(landed[s], 16)

            with sp.Fori(0, LAYERS) as l:
                q0 = sp.snap(sp.snap(extra, min_val=0, max_val=96) + l * EPAIRS, min_val=0, max_val=1000)
                sp.dma_start(gain[:], spread(a["norm1_g"][bass.ds(l, 1), :])).then_inc(d_gain1, 16)
                sp.dma_start(flip, a["c_flip"]).then_inc(d_rel, 16)
                width = 31
                for h in range(4):
                    first = a["na_rpb"][bass.ds(l, 1), h:h + 1, 4:11, 0:GRID // 2 - 1]
                    lo = 15 - (GRID - 1)
                    src = bass.AP(first.tensor, first.offset + lo, [[1, GRID], [width, 7], [1, GRID]])
                    sp.dma_start(relrev[:, h], src).then_inc(d_rel, 16)
                for s in range(3):
                    if s == 2:
                        small_loads(l)
                    lo, hi = SEG[GROUPS[s]][0], SEG[GROUPS[s]][0] + SEG_COLS
                    sp.wait_ge((p_gate, p_up, p_down)[s], q0 * (1, 1, 2)[s] + AHEAD)
                    sp.sem_inc(seen[0], 1)
                    src = a["w_in"][bass.ds(l, 1), :, lo:hi].rearrange("l (p k) c -> (l p) k c", k=KD)
                    sp.dma_start(slot8[s][:, :, 0:hi - lo], src).then_inc(landed[s], 16)
                sp.wait_ge(p_down, q0 * 2 + AHEAD)
                src = a["w_out"][bass.ds(l, 1)].rearrange("l (p k) c -> (l p) k c", k=KD)
                sp.dma_start(slot8[3], src).then_inc(landed[3], 16)
                with sp.Fori(0, EPAIRS // UNROLL) as i4:
                    q4 = sp.snap(q0 + i4 * UNROLL, min_val=0, max_val=1000)
                    for ii in range(UNROLL):
                        free = []
                        for j in range(3):
                            def wait(j=j):
                                before = 3 * ii + j - SLOTS
                                item, kind = before // 3, before % 3
                                per = (1, 1, 2)[kind]
                                value = sp.snap(q4 * per + ((item + 1) * per + AHEAD), min_val=1, max_val=2000)
                                if before < 0:
                                    s = 3 * ii + j
                                    if s < 3:
                                        sp.wait_ge(p_proj, 12 * l + 4 * s + 4)
                                    else:
                                        sp.wait_ge(p_out, 4 * l + 4)
                                    sp.sem_inc(seen[0], 1)
                                sp.wait_ge((p_gate, p_up, p_down)[kind], value)
                            free.append(wait)
                        load_pair(i4 * (2 * UNROLL) + 2 * ii, l, [slot_of(ii, j)[0] for j in range(3)], free)
                sp.wait_ge(v_flags, l + 1)
                sp.sem_inc(seen[0], 1)
                count = sp.value_load(again[0:1, 2 * AGAIN:2 * AGAIN + 1], min_val=0, max_val=AGAIN)
                with sp.If(count):
                    with sp.Fori(0, count) as j:
                        pair = sp.value_load(again[0:1, bass.ds(j, 1)], min_val=0, max_val=EPAIRS - 1)
                        q = sp.snap(sp.snap(extra, min_val=0, max_val=96) + (l + 1) * EPAIRS, min_val=0, max_val=1000)
                        load_pair(pair * 2, l, [0, 1, 2], [
                            lambda: sp.wait_ge(p_gate, q + AHEAD), lambda: sp.wait_ge(p_up, q + AHEAD),
                            lambda: sp.wait_ge(p_down, q * 2 + AHEAD)])
                        sp.reg_add(extra, extra, 1)
            sp.wait_ge(v_x, 2 * LAYERS + 1)
            sp.dma_start(out.rearrange("b (t p) d -> (b p) t d", t=TT), x[:, :, :]).then_inc(d_out, 16)
            sp.wait_ge(d_out, 16)

        @block.gpsimd
        def _(g):
            nc.gpsimd.memset(mhalf[:], -0.5).then_inc(g_init, 1)
            nc.gpsimd.memset(eps[:], EPS).then_inc(g_init, 1)

            def root(n, dst, src, base):
                like = [P, n] if len(src.shape) == 2 else [P, TT, n]
                e = eps[:] if len(like) == 2 else eps[:].unsqueeze(1)
                h = mhalf[:] if len(like) == 2 else mhalf[:].unsqueeze(1)
                nc.gpsimd.tensor_tensor(src, src, e.broadcast_to(like), ALU.add).then_inc(g_step, 1)
                g.wait_ge(g_step, base)
                return nc.gpsimd.tensor_tensor(dst, src, h.broadcast_to(like), ALU.pow)

            g.wait_ge(g_init, 2)
            with g.Fori(0, LAYERS) as l:
                g.wait_ge(a_ss, 3 * l + 1)
                root(TT, rstd[:, 0:TT], ms[:, 0:TT], 6 * l + 1).then_inc(g_rstd, 1)
                nc.gpsimd.memset(keys, 0.0).then_inc(g_keys0, 1)
                for gi, name in enumerate(GROUPS):
                    h0, n = HEAD0[name], SEG[name][3] + SEG[name][4]
                    g.wait_ge(v_ssh, 6 * l + 2 * gi + 2)
                    root(n, rsh[:, :, h0:h0 + n], msh[:, :, h0:h0 + n], 6 * l + 2 + gi).then_inc(g_rstd, 1)
                g.wait_ge(p_s, N_UNITS * l + N_UNITS // 2)
                g.sem_inc(seen[4], 1)
                g.dma_start(gain[:], a["mix_norm_g"][bass.ds(l, 1), :].partition_broadcast(P).rearrange("p a c -> p (a c)")).then_inc(d_gain, 16)
                g.wait_ge(a_ss, 3 * l + 2)
                root(6, rstd[:, 0:6], ms[:, 0:6], 6 * l + 5).then_inc(g_rstd, 1)
                g.wait_ge(v_hn, 6 * l + 4)
                g.sem_inc(seen[4], 1)
                g.dma_start(gain[:], a["norm2_g"][bass.ds(l, 1), :].partition_broadcast(P).rearrange("p a c -> p (a c)")).then_inc(d_gain, 16)
                g.wait_ge(a_ss, 3 * l + 3)
                root(TT, rstd[:, 0:TT], ms[:, 0:TT], 6 * l + 6).then_inc(g_rstd, 1)

        hn_kc = hn[:].rearrange("p t (c k) -> p t k c", k=KD)
        q_c = gain[:].rearrange("p (k s) -> p k s", k=4)

        def queries(pr):
            return q_c[:, pr - 4] if pr >= 4 else hT[:, pr]

        BACK = [(0, 0), (1, 0), (0, 1), (1, 1)]

        Q_BANKS, K_BANK = ((0, 1), (3,), (4,)), (2, 2, 6)
        Q_DONE, K_DONE = ((1, 2), (4,), (6,)), (3, 5, 7)

        @block.tensor
        def _(pe):
            extra = pe.alloc_register("pe_extra")
            pe.reg_mov(extra, 0)
            for s in (p_gather, p_gate, p_up, p_pickT, p_hidT, p_down, p_back):
                pe.sem_inc(s, AHEAD)
            pe.wait_ge(d_first, 32)

            def transposed_rows(l, n):
                pe.wait_ge(v_hn, 6 * l + 2 * n + 2)
                for j in range(4):
                    for kk in range(2):
                        for t in range(TT):
                            c = (2 * kk + t) * P
                            last = nc.tensor.transpose(bank[j][:, c:c + P], hn_kc[:, t, 2 * j + kk, :], ident[:])
                    last.then_inc(p_tr, 1)

            def rows_ready(l, n):
                pe.wait_ge(v_hT, 6 * l + 2 * n + 2)
                pe.wait_ge(a_hT, 6 * l + 2 * n + 2)

            def transposed_heads(l, gi):
                name = GROUPS[gi]
                qo, ko, _, nq, nk = SEG[name]
                pe.wait_ge(v_qk, 3 * l + gi + 1)
                for b, bk in enumerate(Q_BANKS[gi]):
                    for pr in range(2):
                        for t in range(TT):
                            o0 = qo + (2 * b + pr) * P
                            c = (2 * pr + t) * P
                            last = nc.tensor.transpose(bank[bk][:, c:c + P], proj[:, t, o0:o0 + P], ident[:])
                    last.then_inc(p_qk, 1)
                if gi == 1:
                    pe.wait_ge(v_keys, 3 * l + 1)
                for pr in range(2):
                    for t in range(TT):
                        c = (2 * pr + t) * P
                        src = proj[:, t, ko + pr * P:ko + pr * P + P] if name != "C" else \
                            hn[:, t, 640 + pr * P:640 + pr * P + P]
                        last = nc.tensor.transpose(bank[K_BANK[gi]][:, c:c + P], src, ident[:])
                last.then_inc(p_qk, 1)

            def mixers(l, e0):
                pe.wait_ge(d_rel, 80 * (l + 1))
                pe.wait_ge(v_x, 2 * l + 1)
                for h in range(4):
                    nc.tensor.matmul(bank[4 + h][:, 0:7 * GRID], flip, relrev[:, h].rearrange("p r c -> p (r c)"),
                                     start=True, stop=True).then_inc(p_flip, 1)
                transposed_rows(l, 0)
                rows_ready(l, 0)
                for gi, name in enumerate(GROUPS):
                    pe.wait_ge(landed[gi], 16 * (l * USES + 1 + e0))
                    for i in range(4):
                        u, t, c0 = 4 * gi + i, i // 2, i % 2 * HALF_SEG
                        if gi == 0:
                            pe.wait_ge(v_rel, 4 * l + u + 1)
                        else:
                            pe.wait_ge((v_proj, a_proj)[u % 2], 6 * l + (u - 4) // 2 + 1)
                        for k in range(KD):
                            last = nc.tensor.matmul(bank[4 + i][:, 0:HALF_SEG], hT[:, k, t * P:t * P + P],
                                                    slot8[gi][:, k, c0:c0 + HALF_SEG], start=(k == 0), stop=(k == KD - 1))
                        last.then_inc(p_proj, 1)
                    if gi:
                        transposed_heads(l, gi - 1)
                for step in range(N_UNITS + 2):
                    if step == 0:
                        pe.wait_ge(a_q, 4 * l + 2)
                        pe.wait_ge(v_keys, 3 * l + 1)
                    elif step == N_UNITS // 2 - 2:
                        transposed_heads(l, 2)
                    elif step == N_UNITS // 2:
                        pe.wait_ge(a_q, 4 * l + 4)
                        pe.wait_ge(v_keys, 3 * l + 3)
                    u = step
                    if u < N_UNITS:
                        pr, t = ORDER[u // 2], u % 2
                        if u >= 2:
                            pe.wait_ge(a_exp, N_UNITS * l + u - 1)
                        else:
                            pe.wait_ge(a_q, 4 * l + u + 1)
                        nc.tensor.matmul(bank[u % 2][:, :], queries(pr)[:, t * P:t * P + P],
                                         keys[:, KEYPAIR[pr]].rearrange("p h s -> p (h s)"),
                                         start=True, stop=True).then_inc(p_s, 1)
                    u = step - 1
                    if 0 <= u < N_UNITS:
                        pe.wait_ge(a_exp, N_UNITS * l + u + 1)
                        if u >= 2:
                            pe.wait_ge(a_pt, N_UNITS * l + u - 1)
                        elif u == 0:
                            pe.wait_ge(v_keys, 3 * l + 2)
                            pe.wait_ge(a_q, 4 * l + 3)
                        for c in range(4):
                            last = nc.tensor.transpose(bank[2 + u % 2][:, c * P:c * P + P],
                                                       prob[u % 2][:, c * P:c * P + P], ident[:])
                        last.then_inc(p_pt, 1)
                    u = step - 2
                    if u >= 0:
                        pe.wait_ge(a_pt, N_UNITS * l + u + 1)
                        for h in range(2):
                            head, t = 2 * ORDER[u // 2] + h, u % 2
                            if head < 8:
                                vcol = SEG["AB"[head // 4]][2] + head % 4 * HD
                            else:
                                vcol = SEG["C"][2] + (head - 8) // 4 * HD
                            for kt in range(TT):
                                last = nc.tensor.matmul(
                                    bank[4 + 2 * t + head // 8][:, head % 8 * HD:head % 8 * HD + HD],
                                    probT[u % 2][:, (2 * h + kt) * P:(2 * h + kt) * P + P],
                                    proj[:, kt, vcol:vcol + HD], start=(kt == 0), stop=(kt == 1))
                        last.then_inc(p_pv, 1)
                transposed_rows(l, 1)
                rows_ready(l, 1)
                pe.wait_ge(landed[3], 16 * (l * USES + 1))
                for n in range(4):
                    t, half = n // 2, n % 2
                    for k in range(KD):
                        last = nc.tensor.matmul(bank[4 + n][:, :], hT[:, k, t * P:t * P + P],
                                                slot8[3][:, k, half * 512:half * 512 + 512],
                                                start=(k == 0), stop=(k == KD - 1))
                    last.then_inc(p_out, 1)
                transposed_rows(l, 2)
                rows_ready(l, 2)
                pe.wait_ge(d_small, 80 * (l + 1))
                for t in range(TT):
                    for k in range(KD):
                        last = nc.tensor.matmul(bank[4][:, t * 36:t * 36 + 36], hT[:, k, t * P:t * P + P],
                                                w_route[:, k, :], start=(k == 0), stop=(k == KD - 1))
                last.then_inc(p_logit, 1)
                pe.wait_ge(v_chosen, l + 1)
                pe.wait_ge(d_const, 96)
                for c, terms in enumerate((((tri, 0),), ((tri, 1), (ones, 0)), ((ones, 0), (ones, 1)))):
                    for n, (w, t) in enumerate(terms):
                        last = nc.tensor.matmul(bank[5][:, c * NE:c * NE + NE], w[:], chosen[:, t, :],
                                                start=(n == 0), stop=(n == len(terms) - 1))
                last.then_inc(p_rank, 1)

            def gather(gq, pair=None, ps=None):
                pe.wait_ge(v_pick, gq + (AHEAD + 1))
                pe.wait_ge(v_xg, gq + AHEAD)
                pe.wait_ge(a_xg, gq + AHEAD)
                for k in range(KD):
                    n = 0
                    for t in range(TT):
                        for part in range(3):
                            last = nc.tensor.matmul(bank[k // 4][:, k % 4 * P:k % 4 * P + P], xpart[:, part, t, k, :],
                                                    pick[:, t, :], start=(n == 0), stop=(n == 5))
                            n += 1
                    if k % 4 == 3:
                        last.then_inc(p_gather, 1)

            def item(q, gq, slots, rounds, pair, has_next):
                def by_expert(b, weights, k_count, lhs, c0, s, done):
                    for k in range(k_count):
                        for e in range(2):
                            last = nc.tensor.matmul(bank[b][e * CAP:e * CAP + CAP, :], lhs[:, k, e * CAP:e * CAP + CAP],
                                                    weights[s][:, e, k, c0:c0 + 512],
                                                    start=(k == 0), stop=(k == k_count - 1))
                    last.then_inc(done, 1)

                pe.wait_ge(v_xg, gq + (AHEAD + 1))
                pe.wait_ge(a_xg, gq + (AHEAD + 1))
                pe.wait_ge(v_back[0], q + AHEAD)
                pe.wait_ge(landed[slots[0]], rounds[0] * 16 + 16)
                by_expert(2, slot_up, KD, xg, 0, slots[0], p_gate)
                pe.wait_ge(v_back[3], q + AHEAD)
                for t in range(TT):
                    last = nc.tensor.transpose(bank[5][:, t * P:t * P + P], pickw[:, t, :], ident[:])
                last.then_inc(p_pickT, 1)
                pe.wait_ge(v_back[1], q + AHEAD)
                pe.wait_ge(landed[slots[1]], rounds[1] * 16 + 16)
                by_expert(3, slot_up, KD, xg, 0, slots[1], p_up)
                if has_next:
                    gather(gq + 1)
                pe.wait_ge(v_hid, q + (AHEAD + 1))
                pe.wait_ge(v_back[2], q + AHEAD)
                hidc = hid.rearrange("p (f c) -> p c f", c=KE)
                for c in range(KE):
                    last = nc.tensor.transpose(bank[4][:, c * P:c * P + P], hidc[:, c, :], ident[:])
                last.then_inc(p_hidT, 1)
                pe.wait_ge(a_hidT, q + (AHEAD + 1))
                pe.wait_ge(landed[slots[2]], rounds[2] * 16 + 16)
                pe.wait_ge(a_y, q + AHEAD)
                by_expert(6, slot_dn, KE, hidT, 0, slots[2], p_down)
                pe.wait_ge(v_y, q + AHEAD)
                by_expert(7, slot_dn, KE, hidT, 512, slots[2], p_down)
                pe.wait_ge(a_pickT, q + (AHEAD + 1))
                pe.wait_ge(a_y, q + (AHEAD + 1))
                for n, (t, half) in enumerate(BACK):
                    if n == 2:
                        pe.wait_ge(v_y, q + (AHEAD + 1))
                    last = nc.tensor.matmul(bank[2 + n][:, :], pickT[:, t, :], y[:, half * 512:half * 512 + 512],
                                            start=True, stop=True)
                    last.then_inc(p_back, 1)

            run_layers(pe, extra, mixers, gather, item, seen[1])

        @block.scalar
        def _(act):
            extra = act.alloc_register("act_extra")
            act.reg_mov(extra, 0)
            for s in (a_silu, a_pickT, a_xg, a_hidT, a_y):
                act.sem_inc(s, AHEAD)

            act.wait_ge(d_x, 16)
            for name, dst in (("c_rope", rope), ("c_dil", dil), ("c_tri", tri), ("c_ones", ones), ("c_iota", iota), ("c_rev", rev)):
                act.dma_start(dst[:], a[name]).then_inc(d_const, 16)

            def hT_odd_banks(l, n):
                for j in (1, 3):
                    act.wait_ge(p_tr, 12 * l + 4 * n + j + 1)
                    nc.scalar.copy(hT[:, 2 * j:2 * j + 2, :].rearrange("p k s -> p (k s)"), bank[j][:, :]).then_inc(a_hT, 1)

            def mean_squares(l, mark_value):
                act.wait_ge(v_x, mark_value)
                for t in range(TT):
                    last = nc.scalar.activation(hn[:, t, :], x[:, t, :], ACT.Square, scale=D ** -0.5,
                                                accum_out=ms[:, t:t + 1])
                last.then_inc(a_ss, 1)

            def copy_queries(l, gi):
                for b, (bk, n) in enumerate(zip(Q_BANKS[gi], Q_DONE[gi])):
                    act.wait_ge(p_qk, 7 * l + n)
                    dst = q_c[:, 2 * b:2 * b + 2, :] if gi == 0 else hT[:, 2 * gi - 2:2 * gi, :]
                    nc.scalar.copy(dst.rearrange("p k s -> p (k s)"), bank[bk][:, :]).then_inc(a_q, 1)

            def mixers(l, e0):
                mean_squares(l, 2 * l + 1)
                hT_odd_banks(l, 0)
                for gi, name in enumerate(GROUPS):
                    qo, _, vo, _, _ = SEG[name]
                    for t in range(TT):
                        act.wait_ge(p_proj, 12 * l + 4 * gi + 2 * t + 2)
                        nc.scalar.copy(proj[:, t, qo + HALF_SEG:qo + SEG_COLS], bank[5 + 2 * t][:, 0:HALF_SEG]).then_inc(a_proj, 1)
                        act.wait_ge(v_proj, 6 * l + 2 * gi + t + 1)
                        act.wait_ge(a_proj, 6 * l + 2 * gi + t + 1)
                        if gi == 1 and t == 0:
                            act.wait_ge(v_qk, 3 * l + 1)
                        if gi == 2 and t == 0:
                            act.wait_ge(v_ssh, 6 * l + 4)
                        nc.scalar.activation(hn[:, t, 0:vo - qo], proj[:, t, qo:vo], ACT.Square, scale=HD ** -0.5).then_inc(a_sq, 1)
                    if gi == 1:
                        copy_queries(l, 0)
                copy_queries(l, 1)
                for step in range(N_UNITS + 1):
                    u = step
                    if u < N_UNITS:
                        act.wait_ge(v_soft, N_UNITS * l + u + 1)
                        if u >= 2:
                            act.wait_ge(p_pt, N_UNITS * l + u - 1)
                        pr, t = ORDER[u // 2], u % 2
                        for h in range(2):
                            dst = prob[u % 2][:, h * SEQ:h * SEQ + SEQ]
                            src = dst if pr < 4 else bank[u % 2][:, h * SEQ:h * SEQ + SEQ]
                            last = nc.scalar.activation(dst, src, ACT.Exp, bias=nmax[:, u % 2, h:h + 1],
                                                        scale=1.0 if pr < 4 else SCALE,
                                                        accum_out=den[:, t, 2 * pr + h:2 * pr + h + 1])
                        last.then_inc(a_exp, 1)
                    u = step - 1
                    if u >= 0:
                        act.wait_ge(p_pt, N_UNITS * l + u + 1)
                        if u >= 2:
                            act.wait_ge(p_pv, N_UNITS * l + u - 1)
                        nc.scalar.copy(probT[u % 2], bank[2 + u % 2][:, :]).then_inc(a_pt, 1)
                    if step == N_UNITS // 2 - 2:
                        copy_queries(l, 2)
                act.wait_ge(v_o, 4 * l + 4)
                for t in range(TT):
                    for n, (c0, w) in enumerate(((0, 256), (256, 256), (512, 512))):
                        last = nc.scalar.activation(work[:, t * D + c0:t * D + c0 + w], hn[:, t, c0:c0 + w], ACT.Square,
                                                    scale=w ** -0.5, accum_out=ms[:, 3 * t + n:3 * t + n + 1])
                last.then_inc(a_ss, 1)
                hT_odd_banks(l, 1)
                mean_squares(l, 2 * l + 2)
                hT_odd_banks(l, 2)
                act.wait_ge(v_hn, 6 * l + 6)
                for t in range(TT):
                    last = nc.scalar.copy(xpart[:, 0, t], hn_kc[:, t])
                last.then_inc(a_part, 1)
                act.wait_ge(v_router, 2 * l + 1)
                nc.scalar.activation(rb[:, :, 0:NG], ra[:, :, 0:NG], ACT.Exp).then_inc(a_rexp, 1)
                act.wait_ge(v_router, 2 * l + 2)
                nc.scalar.activation(col[:, 4, :], col[:, 3, :], ACT.Exp).then_inc(a_rexp, 1)
                act.wait_ge(v_part, 2 * l + 1)
                for t in range(TT):
                    last = nc.scalar.copy(xpart[:, 1, t], hn_kc[:, t])
                last.then_inc(a_part, 1)

            def gathered(gq, pair=None, ps=None):
                act.wait_ge(p_gather, gq * 2 + (AHEAD + 2))
                nc.scalar.copy(xg[:, 4:8, :].rearrange("p k s -> p (k s)"), bank[1][:, :]).then_inc(a_xg, 1)

            def item(q, gq, slots, rounds, pair, has_next):
                act.wait_ge(p_pickT, q + (AHEAD + 1))
                act.wait_ge(p_back, q * 4 + AHEAD)
                nc.scalar.copy(pickT.rearrange("p t s -> p (t s)"), bank[5][:, 0:2 * P]).then_inc(a_pickT, 1)
                act.wait_ge(p_gate, q + (AHEAD + 1))
                act.wait_ge(p_hidT, q + AHEAD)
                nc.scalar.activation(hid, bank[2][:, :], ACT.Silu).then_inc(a_silu, 1)
                if has_next:
                    act.wait_ge(p_up, q + (AHEAD + 1))
                    gathered(gq + 1)
                act.wait_ge(p_hidT, q + (AHEAD + 1))
                act.wait_ge(p_down, q * 2 + AHEAD)
                nc.scalar.copy(hidT.rearrange("p c s -> p (c s)"), bank[4][:, :]).then_inc(a_hidT, 1)
                act.wait_ge(p_down, q * 2 + (AHEAD + 1))
                nc.scalar.copy(y[:, 0:512], bank[6][:, :]).then_inc(a_y, 1)

            run_layers(act, extra, mixers, gathered, item, seen[2])

        @block.vector
        def _(dve):
            extra = dve.alloc_register("dve_extra")
            dve.reg_mov(extra, 0)
            for s in (v_pick, v_xg, v_hid, v_y, v_istep, *v_back):
                dve.sem_inc(s, AHEAD)
            steps = [0, 0]
            tt, ts, stt = nc.vector.tensor_tensor, nc.vector.tensor_scalar, nc.vector.scalar_tensor_tensor

            def link(ins):
                steps[0] += 1
                ins.then_inc(v_step, 1)
                dve.wait_ge(v_step, steps[1] * V_STEPS + steps[0])

            def wide(ap, n):
                return ap.unsqueeze(len(ap.shape)).broadcast_to(list(ap.shape) + [n])

            def over(ap, axis, n):
                shape = list(ap.shape)
                shape.insert(axis, n)
                return ap.unsqueeze(axis).broadcast_to(shape)

            def hT_even_banks(l, n):
                for j in (0, 2):
                    dve.wait_ge(p_tr, 12 * l + 4 * n + j + 1)
                    nc.vector.tensor_copy(hT[:, 2 * j:2 * j + 2, :].rearrange("p k s -> p (k s)"), bank[j][:, :]).then_inc(v_hT, 1)

            def norm_rows(l, rstd_value, d_sem, gain_value):
                dve.wait_ge(g_rstd, 6 * l + rstd_value)
                dve.wait_ge(d_sem, gain_value)
                for t in range(TT):
                    stt(hn[:, t, :], x[:, t, :], rstd[:, t:t + 1], gain[:], ALU.mult, ALU.mult).then_inc(v_hn, 1)

            def copy_proj(l, gi, t):
                qo = SEG[GROUPS[gi]][0]
                dve.wait_ge(p_proj, 12 * l + 4 * gi + 2 * t + 1)
                nc.vector.tensor_copy(proj[:, t, qo:qo + HALF_SEG], bank[4 + 2 * t][:, 0:HALF_SEG]).then_inc(v_proj, 1)

            def sum_squares(l, gi):
                qo, _, vo, nq, nk = SEG[GROUPS[gi]]
                h0 = HEAD0[GROUPS[gi]]
                for t in range(TT):
                    dve.wait_ge(a_sq, 6 * l + 2 * gi + t + 1)
                    nc.vector.tensor_reduce(msh[:, t, h0:h0 + nq + nk], hn[:, t, 0:vo - qo].rearrange("p (h d) -> p h d", d=HD),
                                            AX_X, ALU.add).then_inc(v_ssh, 1)

            def normalise(l, gi):
                name = GROUPS[gi]
                qo, ko, vo, nq, nk = SEG[name]
                h0 = HEAD0[name]
                dve.wait_ge(a_proj, 6 * l + 2 * gi + 2)
                dve.wait_ge(v_proj, 6 * l + 2 * gi + 2)
                dve.wait_ge(g_rstd, 6 * l + 2 + gi)
                dve.wait_ge(d_small, 80 * (l + 1))
                heads = proj[:, :, qo:vo].rearrange("p t (h d) -> p t h d", d=HD)
                link(tt(heads, heads, wide(rsh[:, :, h0:h0 + nq + nk], HD), ALU.mult))
                qh, kh = heads[:, :, 0:nq, :], heads[:, :, nq:, :]
                which = "ABC".index(name)
                gq = over(over(qkg[:, 2 * which, :], 1, nq), 1, TT)
                gk = over(over(qkg[:, 2 * which + 1, :], 1, nk), 1, TT)
                tt(qh, qh, gq, ALU.mult)
                if name != "C":
                    tt(kh, kh, gk, ALU.mult).then_inc(v_qk, 1)
                    return
                link(tt(kh, kh, gk, ALU.mult))
                dve.wait_ge(d_const, 96)
                part = hn[:, :, 0:(nq + nk) * HD].rearrange("p t (h d) -> p t h d", d=HD)
                for t in range(TT):
                    src = heads[:, t].rearrange("p h (a b f) -> p h a b f", a=2, b=2)
                    dst = part[:, t].rearrange("p h (a b f) -> p h a b f", a=2, b=2)
                    sin = rope[:, t, 1, :].rearrange("p (a b f) -> p a b f", a=2, b=2)
                    for b in range(2):
                        last = tt(dst[:, :, :, b, :], src[:, :, :, 1 - b, :], over(sin[:, :, b, :], 1, nq + nk), ALU.mult)
                link(last)
                for t in range(TT):
                    last = tt(heads[:, t], heads[:, t], over(rope[:, t, 0, :], 1, nq + nk), ALU.mult)
                link(last)
                for t in range(TT):
                    tt(hn[:, t, 640:896].rearrange("p (k c d) -> p k c d", k=nk, c=2),
                       over(heads[:, t, nq:, :], 2, 2), over(part[:, t, nq:, :], 2, 2), ALU.add)
                tt(qh, qh, part[:, :, 0:nq, :], ALU.add).then_inc(v_qk, 1)

            def copy_keys(l, gi):
                j0 = (4, 0, 2)[gi]
                dve.wait_ge(g_keys0, l + 1)
                dve.wait_ge(p_qk, 7 * l + K_DONE[gi])
                for h in range(2):
                    src = bank[K_BANK[gi]][64 * h:64 * h + 64, :].rearrange("p (j s) -> p j s", j=2)
                    last = nc.vector.tensor_copy(keys[64 * h:64 * h + 64, j0:j0 + 2, h, :], src)
                last.then_inc(v_keys, 1)

            def mixers(l, e0):
                steps[0], steps[1] = 0, l
                dve.wait_ge(d_x, 16)
                for n in range(4):
                    dve.wait_ge(v_back[n], l * EPAIRS + e0 + AHEAD)
                nc.vector.memset(mark[:], 0.0).then_inc(v_x, 1)
                norm_rows(l, 1, d_gain1, 16 * l + 16)
                hT_even_banks(l, 0)
                dve.wait_ge(d_first, 32)
                for h in range(4):
                    dve.wait_ge(p_flip, 4 * l + h + 1)
                    tt(rel[:, h], bank[4 + h][:, 0:7 * GRID].rearrange("p (r c) -> p r c", c=GRID),
                       over(colmask[:], 1, 7), ALU.min).then_inc(v_rel, 1)
                for gi in range(3):
                    copy_proj(l, gi, 0)
                    if gi:
                        normalise(l, gi - 1)
                    copy_proj(l, gi, 1)
                    if gi == 2:
                        copy_keys(l, 0)
                    sum_squares(l, gi)
                copy_keys(l, 1)
                dve.wait_ge(v_rel, 4 * l + 4)
                for u in range(N_UNITS):
                    if u == 3:
                        normalise(l, 2)
                    if u == N_UNITS // 2 - 1:
                        copy_keys(l, 2)
                    pr, t = ORDER[u // 2], u % 2
                    dve.wait_ge(p_s, N_UNITS * l + u + 1)
                    if u >= 2:
                        dve.wait_ge(p_pt, N_UNITS * l + u - 1)
                    sc = bank[u % 2][:, :].rearrange("p (h s) -> p h s", h=2)
                    pb = prob[u % 2].rearrange("p (h s) -> p h s", h=2)
                    if pr < 2:
                        for rr in range(2):
                            r = 2 * t + rr
                            rows = slice(64 * rr, 64 * rr + 64)
                            last = stt(pb[rows], sc[rows], SCALE,
                                       rel[rows, 2 * pr:2 * pr + 2, 3 - r:7 - r, :].rearrange("p h r c -> p h (r c)"),
                                       ALU.mult, ALU.add)
                        link(last)
                        nc.vector.tensor_reduce(nmax[:, u % 2, 0:2], pb, AX_X, ALU.max, negate=True).then_inc(v_soft, 1)
                    elif pr < 4:
                        c0 = (1 - t) * P
                        link(stt(pb, sc, SCALE, dil[:, 2 * pr - 4:2 * pr - 2, c0:c0 + SEQ], ALU.mult, ALU.add))
                        nc.vector.tensor_reduce(nmax[:, u % 2, 0:2], pb, AX_X, ALU.max, negate=True).then_inc(v_soft, 1)
                    else:
                        link(nc.vector.tensor_reduce(nmax[:, u % 2, 2:4], sc, AX_X, ALU.max, negate=True))
                        ts(nmax[:, u % 2, 0:2], nmax[:, u % 2, 2:4], SCALE, None, ALU.mult).then_inc(v_soft, 1)
                dve.wait_ge(a_exp, N_UNITS * (l + 1))
                link(nc.vector.reciprocal(rden[:], den[:]))
                dve.wait_ge(p_pv, N_UNITS * (l + 1))
                for t in range(TT):
                    for b in range(2):
                        tt(hn[:, t, b * 512:b * 512 + 512].rearrange("p (h d) -> p h d", d=HD),
                           bank[4 + 2 * t + b][:, :].rearrange("p (h d) -> p h d", d=HD),
                           wide(rden[:, t, 8 * b:8 * b + 8], HD), ALU.mult).then_inc(v_o, 1)
                dve.wait_ge(v_o, 4 * l + 4)
                dve.wait_ge(g_rstd, 6 * l + 5)
                dve.wait_ge(d_gain, 32 * l + 16)
                for t in range(TT):
                    for n, (c0, w) in enumerate(((0, 256), (256, 256), (512, 512))):
                        last = stt(hn[:, t, c0:c0 + w], hn[:, t, c0:c0 + w], rstd[:, 3 * t + n:3 * t + n + 1],
                                   gain[:, c0:c0 + w], ALU.mult, ALU.mult)
                    last.then_inc(v_hn, 1)
                hT_even_banks(l, 1)
                for n in range(4):
                    t, half = n // 2, n % 2
                    dve.wait_ge(p_out, 4 * l + n + 1)
                    xs = x[:, t, half * 512:half * 512 + 512]
                    last = tt(xs, xs, bank[4 + n][:, :], ALU.add)
                last.then_inc(v_x, 1)
                dve.wait_ge(v_x, 2 * l + 2)
                norm_rows(l, 6, d_gain, 32 * l + 32)
                hT_even_banks(l, 2)
                dve.wait_ge(a_part, 2 * l + 1)
                dve.wait_ge(p_tr, 12 * l + 12)
                for t in range(TT):
                    last = tt(hn_kc[:, t], hn_kc[:, t], xpart[:, 0, t], ALU.subtract)
                last.then_inc(v_part, 1)
                dve.wait_ge(p_logit, l + 1)
                dve.wait_ge(d_small, 80 * (l + 1))
                link(tt(lg[:], bank[4][:, 0:72].rearrange("p (t n) -> p t n", t=TT), over(b_route[:], 1, TT), ALU.add))
                gl, el = lg[:, :, 0:NG], lg[:, :, NG:36]
                link(nc.vector.tensor_reduce(col[:, 0, :], gl, AX_X, ALU.max))
                tt(ra[:, :, 0:NG], gl, wide(col[:, 0, :], NG), ALU.subtract).then_inc(v_router, 1)
                dve.wait_ge(v_router, 2 * l + 1)

                def first_of_max(dst, score, diff, n, r0, c):
                    link(stt(score, diff, 0.0, over(rev[:, r0:r0 + n], 1, TT), ALU.is_equal, ALU.mult))
                    link(nc.vector.tensor_reduce(col[:, c, :], score, AX_X, ALU.max))
                    link(tt(dst, score, wide(col[:, c, :], n), ALU.is_equal))

                first_of_max(ra[:, :, 8:12], ra[:, :, 4:8], ra[:, :, 0:NG], NG, 0, 1)
                link(ts(ra[:, :, 12:16], ra[:, :, 8:12], BIG, -BIG, ALU.mult, ALU.add))
                link(tt(el.rearrange("p t (g e) -> p t g e", g=NG), el.rearrange("p t (g e) -> p t g e", g=NG),
                        wide(ra[:, :, 12:16], EPG), ALU.add))
                link(nc.vector.tensor_reduce(col[:, 1, :], el, AX_X, ALU.max))
                dve.wait_ge(a_rexp, 2 * l + 1)
                link(nc.vector.tensor_reduce(col[:, 5, :], rb[:, :, 0:NG], AX_X, ALU.add))
                link(tt(ra[:, :, 4:36], el, wide(col[:, 1, :], NE), ALU.subtract))
                first_of_max(oh1[:], rb[:, :, 4:36], ra[:, :, 4:36], NE, 4, 6)
                link(stt(el, oh1[:], -BIG, el, ALU.mult, ALU.add))
                link(nc.vector.tensor_reduce(col[:, 2, :], el, AX_X, ALU.max))
                tt(col[:, 3, :], col[:, 2, :], col[:, 1, :], ALU.subtract).then_inc(v_router, 1)
                link(tt(ra[:, :, 4:36], el, wide(col[:, 2, :], NE), ALU.subtract))
                first_of_max(oh2[:], rb[:, :, 4:36], ra[:, :, 4:36], NE, 4, 6)
                tt(chosen[:], oh1[:], oh2[:], ALU.add).then_inc(v_chosen, 1)
                link(nc.vector.reciprocal(col[:, 7, :], col[:, 5, :]))
                dve.wait_ge(a_rexp, 2 * l + 2)
                link(ts(col[:, 8, :], col[:, 4, :], 1.0, None, ALU.add))
                link(nc.vector.reciprocal(col[:, 9, :], col[:, 8, :]))
                link(tt(col[:, 10, :], col[:, 9, :], col[:, 7, :], ALU.mult))
                link(tt(col[:, 11, :], col[:, 10, :], col[:, 4, :], ALU.mult))
                tt(oh1[:], oh1[:], wide(col[:, 10, :], NE), ALU.mult)
                link(tt(oh2[:], oh2[:], wide(col[:, 11, :], NE), ALU.mult))
                tt(rg[:, TT:2 * TT, 0:NE], oh1[:], oh2[:], ALU.add)
                nc.vector.memset(rg[:, :, NE:], -1.0)
                dve.wait_ge(p_rank, l + 1)
                dve.wait_ge(v_chosen, l + 1)
                link(stt(rb[:, :, 0:NE], bank[5][:, 0:2 * NE].rearrange("p (t n) -> p t n", t=TT), 1.0, chosen[:],
                         ALU.add, ALU.mult))
                link(ts(rg[:, 0:TT, 0:NE], rb[:, :, 0:NE], -1.0, None, ALU.add))
                counts = bank[5][0:1, 2 * NE:3 * NE].rearrange("p (j e) -> p j e", e=2)
                link(nc.vector.tensor_reduce(pairmax[:], counts, AX_X, ALU.max))
                dve.wait_ge(a_part, 2 * l + 2)
                for t in range(TT):
                    last = tt(xpart[:, 2, t], hn_kc[:, t], xpart[:, 1, t], ALU.subtract)
                last.then_inc(v_part, 1)

            def list_again():
                n = (PASSES - 1) * EPAIRS
                rank, score = (m[0:1].rearrange("p t h -> p (t h)")[:, 0:n] for m in (msh, rsh))
                top, idx, run, nonzero = (den[0:1].rearrange("p t h -> p (t h)")[:, i * AGAIN:i * AGAIN + AGAIN] for i in range(4))
                link(ts(rank, iota[0:1, 0:n], -1.0, float(n), ALU.mult, ALU.add))
                for ps in range(PASSES - 1):
                    part = slice(ps * EPAIRS, ps * EPAIRS + EPAIRS)
                    last = stt(score[:, part], pairmax[:], float(CAP * (ps + 1)), rank[:, part], ALU.is_gt, ALU.mult)
                link(last)
                dve.sem_inc(seen[3], 1)
                link(nc.vector.max(top, score))
                ts(nonzero, top, 0.0, None, ALU.is_gt)
                link(ts(idx, top, -1.0, float(n), ALU.mult, ALU.add))
                link(ts(run, idx, EPAIRS - 0.5, None, ALU.is_gt))
                link(stt(run, idx, 2 * EPAIRS - 0.5, run, ALU.is_gt, ALU.add))
                stt(again[:, 0:AGAIN], run, -float(EPAIRS), idx, ALU.mult, ALU.add)
                nc.vector.tensor_copy(again[:, AGAIN:2 * AGAIN], run)
                link(nc.vector.tensor_reduce(rden[0:1, 0, 0:1], nonzero, AX_X, ALU.add))
                nc.vector.tensor_copy(again[:, 2 * AGAIN:2 * AGAIN + 1], rden[0:1, 0, 0:1]).then_inc(v_flags, 1)
                assert steps[0] == V_STEPS, steps

            def picks(gq, pair, ps):
                nc.vector.tensor_copy(rgc[:], rg[:, :, bass.ds(pair * 2, 2)] if not isinstance(pair, int)
                                      else rg[:, :, 2 * pair:2 * pair + 2]).then_inc(v_istep, 1)
                dve.wait_ge(v_istep, gq * 2 + (AHEAD + 1))
                places = iota[:, 0:CAP] if ps is None else iota[:, bass.ds(ps * CAP + CAP, CAP)]
                hot = pick.rearrange("p t (e s) -> p (t e) s", e=2)
                tt(hot, over(places, 1, 2 * TT), wide(rgc[:, 0:TT, :].rearrange("p t e -> p (t e)"), CAP),
                   ALU.is_equal).then_inc(v_istep, 1)
                dve.wait_ge(v_istep, gq * 2 + (AHEAD + 2))
                tt(pickw.rearrange("p t (e s) -> p (t e) s", e=2), hot,
                   wide(rgc[:, TT:2 * TT, :].rearrange("p t e -> p (t e)"), CAP), ALU.mult).then_inc(v_pick, 1)

            def copy_gathered(gq):
                dve.wait_ge(p_gather, gq * 2 + (AHEAD + 1))
                nc.vector.tensor_copy(xg[:, 0:4, :].rearrange("p k s -> p (k s)"), bank[0][:, :]).then_inc(v_xg, 1)

            def first(gq, pair, ps):
                picks(gq, pair, ps)
                if ps is None:
                    list_again()
                copy_gathered(gq)

            def item(q, gq, slots, rounds, pair, has_next):
                if has_next:
                    dve.wait_ge(p_pickT, q + (AHEAD + 1))
                    picks(gq + 1, pair + 1, None)
                dve.wait_ge(a_silu, q + (AHEAD + 1))
                dve.wait_ge(p_up, q + (AHEAD + 1))
                tt(hid, hid, bank[3][:, :], ALU.mult).then_inc(v_hid, 1)
                if has_next:
                    copy_gathered(gq + 1)
                dve.wait_ge(p_down, q * 2 + (AHEAD + 2))
                dve.wait_ge(p_back, q * 4 + AHEAD)
                nc.vector.tensor_copy(y[:, 512:1024], bank[7][:, :]).then_inc(v_y, 1)
                for n, (t, half) in enumerate(BACK):
                    dve.wait_ge(p_back, q * 4 + (AHEAD + n + 1))
                    dve.wait_ge(v_back[n], q + AHEAD)
                    xs = x[:, t, half * 512:half * 512 + 512]
                    tt(xs, xs, bank[2 + n][:, :], ALU.add).then_inc(v_back[n], 1)

            run_layers(dve, extra, mixers, first, item, seen[3])
            e = dve.snap(extra, min_val=0, max_val=96)
            for n in range(4):
                dve.wait_ge(v_back[n], e + (LAYERS * EPAIRS + AHEAD))
            nc.vector.memset(mark[:], 0.0).then_inc(v_x, 1)


_INS = ["x", "norm1_g", "w_in", "qk_norm_g", "na_rpb", "mix_norm_g", "w_out", "norm2_g", "w_router_group",
        "b_router_group", "w_router_expert", "b_router_expert", "w_gate", "w_up", "w_down"]


def shape_constants():
    t = np.arange(SEQ)
    nf = HD // 4
    inv = (10000.0 ** (-np.arange(nf, dtype=np.float32) / nf)).astype(np.float32)
    ang = np.stack([(t // GRID).astype(np.float32)[:, None] * inv, (t % GRID).astype(np.float32)[:, None] * inv], 1)
    cos = np.repeat(np.cos(ang)[:, :, None, :], 2, axis=2).reshape(SEQ, HD)
    sin = np.stack([-np.sin(ang), np.sin(ang)], axis=2).reshape(SEQ, HD)
    rope = np.stack([cos, sin], 1).reshape(TT, P, 2, HD).transpose(1, 0, 2, 3)
    c = np.arange(P)[:, None] % GRID
    start = np.clip(c - 8, 0, GRID - 16)
    kc = np.arange(GRID)[None, :]
    colmask = np.where((kc >= start) & (kc < start + 16), 3e38, -BIG)
    dist = np.abs(np.arange(P)[:, None] - (np.arange(3 * P)[None, :] - P))
    count = (dist <= 64).astype(int) + ((dist % 4 == 0) & (dist <= 256)) + ((dist % 16 == 0) & (dist <= 1024))
    slope = 2.0 ** (-8.0 * np.arange(1, 5) / 4)
    base = np.where(count > 0, np.log(np.maximum(count, 1)), -BIG)
    dil = base[:, None, :] - slope[None, :, None] * dist[:, None, :] * (count > 0)[:, None, :]
    return {
        "c_rope": np.ascontiguousarray(rope, np.float32), "c_colmask": colmask.astype(np.float32),
        "c_flip": np.tile(np.eye(GRID, dtype=np.float32)[::-1], (1, 2)),
        "c_ident": np.eye(P, dtype=np.float32), "c_dil": dil.astype(np.float32),
        "c_tri": np.triu(np.ones((P, P)), 1), "c_ones": np.ones((P, P)),
        "c_iota": np.tile(np.arange(SEQ, dtype=np.float32), (P, 1)),
        "c_rev": np.tile(np.concatenate([np.arange(4, 0, -1), np.arange(32, 0, -1)]).astype(np.float32), (P, 1)),
    }


def kernel(**inputs):
    import ml_dtypes
    import concourse.bacc as _bacc
    from concourse import mybir as _mybir
    from concourse.bass_utils import run_bass_kernel_spmd as _run

    nc = _bacc.Bacc("TRN2", target_bir_lowering=False, num_devices=1)
    arrays, aps = {}, {}
    consts = shape_constants()
    for name in ("c_tri", "c_ones"):
        consts[name] = consts[name].astype(ml_dtypes.bfloat16)
    for name, value in list({n: inputs[n] for n in _INS}.items()) + list(consts.items()):
        v = np.ascontiguousarray(value)
        arrays[f"in_{name}"] = v
        aps[name] = nc.dram_tensor(f"in_{name}", v.shape, _mybir.dt.from_np(v.dtype), kind="ExternalInput").ap()
    out = nc.dram_tensor("out", (1, SEQ, D), _mybir.dt.float32, kind="ExternalOutput").ap()
    encoder(nc, aps, out)
    r = _run(nc, [arrays], core_ids=[0])
    return r.results[0]["out"]
```

```python
from contextlib import ExitStack

import numpy as np

import concourse.bass as bass
from concourse import mybir

F32 = mybir.dt.float32
BF16 = mybir.dt.bfloat16
I32 = mybir.dt.int32
ALU = mybir.AluOpType
ACT = mybir.ActivationFunctionType
AX_X = mybir.AxisListType.X

P = 128
LAYERS = 2
SEQ, D = 256, 1024
TT = SEQ // P
KD = D // P
HD = 64
IN_COLS = 2304
EPS = 1e-6
BIG = 1e30
GRID = 64
SCALE = HD ** -0.5

SEG = {"A": (0, 256, 512, 4, 4), "B": (768, 1024, 1280, 4, 4), "C": (1536, 2048, 2176, 8, 2)}
HEAD0 = {"A": 0, "B": 8, "C": 16}
NHEAD = 26
GROUPS = ("C", "A", "B")
SEG_COLS = 768
HALF_SEG = SEG_COLS // 2
PAIRS = 8
UNITS = [(pr, t) for prs in ((4, 5, 6, 7), (0, 1, 2, 3)) for t in range(TT) for pr in prs]
N_UNITS = len(UNITS)
TILE0_UNITS = N_UNITS - 4
KEYPAIR = [0, 1, 2, 3, 4, 4, 5, 5]

NG, NE, EPG = 4, 32, 8
DE = 512
KE = DE // P
CAP = 64
EPAIRS = NE // 2
PASSES = SEQ // CAP
AGAIN = 8
UNROLL = 4
AHEAD = 3
SLOT = 8192
SLOTS = 4
MIX_USES = 1
MOE_USES = 3 * EPAIRS // SLOTS
USES = MIX_USES + MOE_USES

PROJ = TT * IN_COLS
KEYS = 6 * 2 * SEQ
WORK = PROJ + KEYS


def encoder(nc, a, out):
    ctx = ExitStack()
    with ctx:
        def sb(name, shape, dt=F32):
            return ctx.enter_context(nc.sbuf_tensor(name, shape, dt))

        def sem(name):
            return ctx.enter_context(nc.semaphore(name))

        ring = [sb(f"ring{i}", [P, SLOT]) for i in range(SLOTS)]
        x = sb("x", [P, TT, D])
        hn = sb("hn", [P, TT, D])
        hT = sb("hT", [P, KD, SEQ])
        work = sb("work", [P, WORK])
        rel = sb("rel", [P, 4, 7, GRID])
        dil = sb("dil", [P, 4, 3 * P])
        gain = sb("gain", [P, D])
        qkg = sb("qkg", [P, 6, HD])
        rope = sb("rope", [P, TT, 2, HD])
        colmask = sb("colmask", [P, GRID])
        ident = sb("ident", [P, P])
        tri = sb("tri", [P, P], BF16)
        ones = sb("ones", [P, P], BF16)
        iota = sb("iota", [P, SEQ])
        rev = sb("rev", [P, 36])
        w_route = sb("w_route", [P, KD, 36])
        b_route = sb("b_route", [P, 36])
        ms = sb("ms", [P, 8])
        rstd = sb("rstd", [P, 8])
        msh = sb("msh", [P, TT, NHEAD])
        rsh = sb("rsh", [P, TT, NHEAD])
        mhalf = sb("mhalf", [P, 1])
        eps = sb("eps", [P, 1])
        nmax = sb("nmax", [P, 3, 4])
        den = sb("den", [P, TT, 16])
        rden = sb("rden", [P, TT, 16])
        col = sb("col", [P, 12, TT])
        rg = sb("rg", [P, 2 * TT, NE + 2])
        rgc = sb("rgc", [P, 2 * TT, 2])
        again = sb("again", [1, 2 * AGAIN + 1], I32)
        pairmax = sb("pairmax", [1, EPAIRS])
        mark = sb("mark", [1, 8])

        proj = work[:, 0:PROJ].rearrange("p (t c) -> p t c", t=TT)
        keys = work[:, PROJ:WORK].rearrange("p (j h s) -> p j h s", j=6, h=2)
        prob = [work[:, c:c + 512] for c in (0, IN_COLS)] + [hn[:, 1, 0:512]]
        squares = [work[:, c + SEG["B"][0]:c + SEG["B"][0] + 512] for c in (0, IN_COLS)]
        probT = [work[:, c + SEG["C"][0]:c + SEG["C"][0] + 512] for c in (0, IN_COLS)]
        o = [0]

        def carve(n):
            o[0] += n
            return work[:, o[0] - n:o[0]]

        xpart = carve(3 * TT * D // 2).bitcast(BF16).rearrange("p (i t k c) -> p i t k c", i=3, t=TT, k=KD)
        pick = carve(TT * P // 2).bitcast(BF16).rearrange("p (t s) -> p t s", t=TT)
        pickw = carve(TT * P).rearrange("p (t s) -> p t s", t=TT)
        pickT = carve(TT * P).rearrange("p (t s) -> p t s", t=TT)
        xg = carve(KD * P).rearrange("p (k s) -> p k s", k=KD)
        hid = carve(DE)
        hidT = carve(DE).rearrange("p (c s) -> p c s", c=KE)
        y = carve(D)
        lg, ra, rb = (carve(TT * 36).rearrange("p (t n) -> p t n", t=TT) for _ in range(3))
        oh1, oh2 = (carve(TT * NE).rearrange("p (t n) -> p t n", t=TT) for _ in range(2))
        chosen = carve(TT * NE // 2).bitcast(BF16).rearrange("p (t n) -> p t n", t=TT)
        hT_flat = hT[:].rearrange("p k s -> p (k s)")
        flip = hT_flat[0:GRID, 0:P]
        relrev = hT_flat[0:GRID, P:P + 28 * GRID].rearrange("p (h r c) -> p h r c", h=4, r=7)

        bank = [ctx.enter_context(nc.psum_tensor(f"bank{i}", [P, 512], F32)) for i in range(8)]

        d_x, d_first, d_const, d_rel = sem("d_x"), sem("d_first"), sem("d_const"), sem("d_rel")
        d_gain1, d_gain, d_small, d_out = sem("d_gain1"), sem("d_gain"), sem("d_small"), sem("d_out")
        landed = [[sem(f"landed{i}_{half}") for half in range(2)] for i in range(SLOTS)]
        p_tr, p_proj, p_qk, p_s, p_pt, p_pv = (sem("p_" + n) for n in ("tr", "proj", "qk", "s", "pt", "pv"))
        p_out, p_logit, p_rank, p_flip = sem("p_out"), sem("p_logit"), sem("p_rank"), sem("p_flip")
        p_gather, p_gate, p_up, p_pickT, p_hidT, p_down, p_back = (
            sem("p_" + n) for n in ("gather", "gate", "up", "pickT", "hidT", "down", "back"))
        a_ss, a_hT, a_proj, a_sq, a_q, a_exp, a_pt = (sem("a_" + n) for n in ("ss", "hT", "proj", "sq", "q", "exp", "pt"))
        a_rexp, a_part, a_silu, a_pickT, a_xg, a_hidT, a_y = (
            sem("a_" + n) for n in ("rexp", "part", "silu", "pickT", "xg", "hidT", "y"))
        v_x, v_hn, v_hT, v_proj, v_ssh, v_qk, v_keys, v_soft = (
            sem("v_" + n) for n in ("x", "hn", "hT", "proj", "ssh", "qk", "keys", "soft"))
        v_rel = sem("v_rel")
        v_o, v_router, v_chosen, v_flags, v_res, v_part, v_step = (
            sem("v_" + n) for n in ("o", "router", "chosen", "flags", "res", "part", "step"))
        v_pick, v_pickw, v_xg, v_hid, v_y, v_istep = (sem("v_" + n) for n in ("pick", "pickw", "xg", "hid", "y", "istep"))
        v_back = [sem(f"v_back{n}") for n in range(4)]
        g_init, g_rstd, g_step, g_keys0, g_part = (sem("g_" + n) for n in ("init", "rstd", "step", "keys0", "part"))
        seen = [sem(f"seen{i}") for i in range(5)]

        slot8 = [r[:, :].rearrange("p (k c) -> p k c", k=KD) for r in ring]
        slot_up = [r[:, :].rearrange("p (e k c) -> p e k c", e=2, k=KD) for r in ring]
        slot_dn = [r[:, :].rearrange("p (e k c) -> p e k c", e=2, k=KE) for r in ring]
        V_STEPS = 60

        def slot_of(i, j):
            u = 3 * i + j
            return u % SLOTS, u // SLOTS

        def run_layers(eng, extra, mixers, first, item, seen_sem):
            with eng.Fori(0, LAYERS) as l:
                e0 = eng.snap(extra, min_val=0, max_val=96)
                mixers(l, e0)
                first(eng.snap(l * (EPAIRS + 1) + e0, min_val=0, max_val=1000), 0, None)
                with eng.Fori(0, EPAIRS // UNROLL) as i4:
                    for ii in range(UNROLL):
                        q = eng.snap(l * EPAIRS + e0 + i4 * UNROLL + ii, min_val=0, max_val=1000)
                        so = [slot_of(ii, j) for j in range(3)]
                        rounds = [i4 * 3 + l * USES + (MIX_USES + r) + (e0 if s < 3 else 0) for s, r in so]
                        item(q, q + l, [s for s, _ in so], rounds, i4 * UNROLL + ii, True)
                eng.wait_ge(v_flags, l + 1)
                eng.sem_inc(seen_sem, 1)
                count = eng.value_load(again[0:1, 2 * AGAIN:2 * AGAIN + 1], min_val=0, max_val=AGAIN)
                with eng.If(count):
                    with eng.Fori(0, count) as j:
                        pair = eng.value_load(again[0:1, bass.ds(j, 1)], min_val=0, max_val=EPAIRS - 1)
                        ps = eng.value_load(again[0:1, bass.ds(j + AGAIN, 1)], min_val=0, max_val=PASSES - 2)
                        e = eng.snap(extra, min_val=0, max_val=96)
                        q = eng.snap(l * EPAIRS + EPAIRS + e, min_val=0, max_val=1000)
                        gq = eng.snap(q + l + 1, min_val=0, max_val=1000)
                        first(gq, pair, ps)
                        item(q, gq, [0, 1, 2], [l * USES + USES + e] * 3, pair, False)
                        eng.reg_add(extra, extra, 1)

        block = ctx.enter_context(nc.Block())

        @block.sync
        def _(sp):
            extra = sp.alloc_register("sp_extra")
            sp.reg_mov(extra, 0)
            xr = a["x"].rearrange("b (t p) d -> (b p) t d", t=TT)
            sp.dma_start(x[:, :, :], xr).then_inc(d_x, 16)
            for name, dst in (("c_ident", ident), ("c_colmask", colmask)):
                sp.dma_start(dst[:], a[name]).then_inc(d_first, 16)

            def spread(src):
                return src.partition_broadcast(P).rearrange("p a c -> p (a c)")

            def small_loads(l):
                sp.dma_start(qkg[:], a["qk_norm_g"][bass.ds(l, 1)].rearrange("l m q d -> l (m q) d").partition_broadcast(P)
                             .rearrange("p l m d -> p (l m) d")).then_inc(d_small, 16)
                for w_name, b_name, lo, hi in (("w_router_group", "b_router_group", 0, NG),
                                               ("w_router_expert", "b_router_expert", NG, 36)):
                    sp.dma_start(w_route[:, :, lo:hi], a[w_name][bass.ds(l, 1)].rearrange("l (p k) n -> (l p) k n", k=KD)).then_inc(d_small, 16)
                    sp.dma_start(b_route[:, lo:hi], spread(a[b_name][bass.ds(l, 1), :])).then_inc(d_small, 16)

            def load_pair(pair, l, slots, free):
                for j, name in enumerate(("w_gate", "w_up", "w_down")):
                    s = slots[j]
                    k = KE if name == "w_down" else KD
                    dst = slot_dn[s] if name == "w_down" else slot_up[s]
                    for half in range(2):
                        free[j](half)
                        ks = slice(half * k // 2, half * k // 2 + k // 2)
                        src = a[name][bass.ds(l, 1), bass.ds(pair, 2)].rearrange("l e (p k) c -> p (l e) k c", k=k)
                        sp.dma_start(dst[:, :, ks], src[:, :, ks]).then_inc(landed[s][half], 16)

            with sp.Fori(0, LAYERS) as l:
                q0 = sp.snap(sp.snap(extra, min_val=0, max_val=96) + l * EPAIRS, min_val=0, max_val=1000)
                sp.dma_start(gain[:], spread(a["norm1_g"][bass.ds(l, 1), :])).then_inc(d_gain1, 16)
                sp.dma_start(flip, a["c_flip"]).then_inc(d_rel, 16)
                width = 31
                for h in range(4):
                    first = a["na_rpb"][bass.ds(l, 1), h:h + 1, 4:11, 0:GRID // 2 - 1]
                    lo = 15 - (GRID - 1)
                    src = bass.AP(first.tensor, first.offset + lo, [[1, GRID], [width, 7], [1, GRID]])
                    sp.dma_start(relrev[:, h], src).then_inc(d_rel, 16)
                for s in range(3):
                    if s == 2:
                        with sp.If(sp.snap(l * -1 + 1, min_val=0, max_val=1)):
                            for name, dst in (("c_rope", rope), ("c_dil", dil), ("c_tri", tri), ("c_ones", ones),
                                              ("c_iota", iota), ("c_rev", rev)):
                                sp.dma_start(dst[:], a[name]).then_inc(d_const, 16)
                        small_loads(l)
                    lo = SEG[GROUPS[s]][0]
                    sp.wait_ge((p_gate, p_up, p_down)[s], q0 * (2, 1, 2)[s] + AHEAD)
                    sp.sem_inc(seen[0], 1)
                    for half in range(2):
                        c0 = half * HALF_SEG
                        src = a["w_in"][bass.ds(l, 1), :, lo + c0:lo + c0 + HALF_SEG].rearrange("l (p k) c -> (l p) k c", k=KD)
                        sp.dma_start(slot8[s][:, :, c0:c0 + HALF_SEG], src).then_inc(landed[s][half], 16)
                sp.wait_ge(p_down, q0 * 2 + AHEAD)
                for half in range(2):
                    cols = slice(half * 512, half * 512 + 512)
                    src = a["w_out"][bass.ds(l, 1), :, cols].rearrange("l (p k) c -> (l p) k c", k=KD)
                    sp.dma_start(slot8[3][:, :, cols], src).then_inc(landed[3][half], 16)
                with sp.Fori(0, EPAIRS // UNROLL) as i4:
                    q4 = sp.snap(q0 + i4 * UNROLL, min_val=0, max_val=1000)
                    for ii in range(UNROLL):
                        free = []
                        for j in range(3):
                            def wait(half, j=j):
                                before = 3 * ii + j - SLOTS
                                item, kind = before // 3, before % 3
                                per = (2, 1, 2)[kind]
                                early = 1 - half if kind == 0 else 0
                                value = sp.snap(q4 * per + ((item + 1) * per + AHEAD - early), min_val=1, max_val=2000)
                                if before < 0 and half == 0:
                                    s = 3 * ii + j
                                    if s < 3:
                                        sp.wait_ge(p_proj, 12 * l + 4 * s + 4)
                                    else:
                                        sp.wait_ge(p_out, 4 * l + 4)
                                    sp.sem_inc(seen[0], 1)
                                sp.wait_ge((p_gate, p_up, p_down)[kind], value)
                            free.append(wait)
                        load_pair(i4 * (2 * UNROLL) + 2 * ii, l, [slot_of(ii, j)[0] for j in range(3)], free)
                sp.wait_ge(v_flags, l + 1)
                sp.sem_inc(seen[0], 1)
                count = sp.value_load(again[0:1, 2 * AGAIN:2 * AGAIN + 1], min_val=0, max_val=AGAIN)
                with sp.If(count):
                    with sp.Fori(0, count) as j:
                        pair = sp.value_load(again[0:1, bass.ds(j, 1)], min_val=0, max_val=EPAIRS - 1)
                        q = sp.snap(sp.snap(extra, min_val=0, max_val=96) + (l + 1) * EPAIRS, min_val=0, max_val=1000)
                        load_pair(pair * 2, l, [0, 1, 2], [
                            lambda half: sp.wait_ge(p_gate, q * 2 + AHEAD), lambda half: sp.wait_ge(p_up, q + AHEAD),
                            lambda half: sp.wait_ge(p_down, q * 2 + AHEAD)])
                        sp.reg_add(extra, extra, 1)
            sp.wait_ge(v_x, 3 * LAYERS + 1)
            sp.dma_start(out.rearrange("b (t p) d -> (b p) t d", t=TT), x[:, :, :]).then_inc(d_out, 16)
            sp.wait_ge(d_out, 16)

        hn_kc = hn[:].rearrange("p t (c k) -> p t k c", k=KD)

        @block.gpsimd
        def _(g):
            nc.gpsimd.memset(mhalf[:], -0.5).then_inc(g_init, 1)
            nc.gpsimd.memset(eps[:], EPS).then_inc(g_init, 1)

            def root(n, dst, src, base):
                like = [P, n] if len(src.shape) == 2 else [P, TT, n]
                e = eps[:] if len(like) == 2 else eps[:].unsqueeze(1)
                h = mhalf[:] if len(like) == 2 else mhalf[:].unsqueeze(1)
                nc.gpsimd.tensor_tensor(src, src, e.broadcast_to(like), ALU.add).then_inc(g_step, 1)
                g.wait_ge(g_step, base)
                return nc.gpsimd.tensor_tensor(dst, src, h.broadcast_to(like), ALU.pow)

            g.wait_ge(g_init, 2)
            with g.Fori(0, LAYERS) as l:
                g.wait_ge(a_ss, 5 * l + 1)
                root(TT, rstd[:, 0:TT], ms[:, 0:TT], 8 * l + 1).then_inc(g_rstd, 1)
                nc.gpsimd.memset(keys, 0.0).then_inc(g_keys0, 1)
                for gi, name in enumerate(GROUPS):
                    h0, n = HEAD0[name], SEG[name][3] + SEG[name][4]
                    g.wait_ge(v_ssh, 6 * l + 2 * gi + 2)
                    root(n, rsh[:, :, h0:h0 + n], msh[:, :, h0:h0 + n], 8 * l + 2 + gi).then_inc(g_rstd, 1)
                g.wait_ge(p_s, N_UNITS * l + N_UNITS // 2)
                g.sem_inc(seen[4], 1)
                g.dma_start(gain[:], a["mix_norm_g"][bass.ds(l, 1), :].partition_broadcast(P).rearrange("p a c -> p (a c)")).then_inc(d_gain, 16)
                for m in range(4):
                    g.wait_ge(a_ss, 5 * l + 2 + m)
                    c, n = ((0, 3), (3, 3), (6, 1), (7, 1))[m]
                    root(n, rstd[:, c:c + n], ms[:, c:c + n], 8 * l + 5 + m).then_inc(g_rstd, 1)
                    if m == 1:
                        g.wait_ge(v_hn, 6 * l + 4)
                        g.sem_inc(seen[4], 1)
                        g.dma_start(gain[:], a["norm2_g"][bass.ds(l, 1), :].partition_broadcast(P).rearrange("p a c -> p (a c)")).then_inc(d_gain, 16)
                g.wait_ge(a_part, 3 * l + 3)
                for t in range(TT):
                    last = nc.gpsimd.tensor_tensor(xpart[:, 2, t], hn_kc[:, t], xpart[:, 1, t], ALU.subtract)
                last.then_inc(g_part, 1)

        TILE_STAGES = ((0, 4), (1, 6), (0, 4), (1, 6))
        q_c = gain[:].rearrange("p (k s) -> p k s", k=4)

        def queries(pr):
            return q_c[:, pr - 4] if pr >= 4 else hT[:, pr]

        BACK = [(0, 0), (1, 0), (0, 1), (1, 1)]

        Q_BANKS, K_BANK = ((0, 1), (3,), (4,)), (2, 2, 6)
        Q_DONE, K_DONE = ((1, 2), (4,), (6,)), (3, 5, 7)

        @block.tensor
        def _(pe):
            extra = pe.alloc_register("pe_extra")
            pe.reg_mov(extra, 0)
            for s in (p_gather, p_gate, p_up, p_pickT, p_hidT, p_down, p_back):
                pe.sem_inc(s, AHEAD)
            pe.wait_ge(d_first, 32)

            def transposed_rows(l):
                pe.wait_ge(v_hn, 6 * l + 2)
                for j in range(4):
                    for kk in range(2):
                        for t in range(TT):
                            c = (2 * kk + t) * P
                            last = nc.tensor.transpose(bank[j][:, c:c + P], hn_kc[:, t, 2 * j + kk, :], ident[:])
                    last.then_inc(p_tr, 1)

            def transposed_tile(l, m):
                t, b0 = TILE_STAGES[m]
                pe.wait_ge(v_hn, 6 * l + 3 + m)
                for j in range(2):
                    for kk in range(4):
                        last = nc.tensor.transpose(bank[b0 + j][:, kk * P:kk * P + P], hn_kc[:, t, 4 * j + kk, :], ident[:])
                    last.then_inc(p_tr, 1)

            def tile_ready(l, m):
                pe.wait_ge(v_hT, 6 * l + 3 + m)
                pe.wait_ge(a_hT, 6 * l + 3 + m)

            def scores(l, u):
                pr, t = UNITS[u]
                if u >= 3:
                    pe.wait_ge(a_exp, N_UNITS * l + u - 2)
                nc.tensor.matmul(bank[u % 3][:, :], queries(pr)[:, t * P:t * P + P],
                                 keys[:, KEYPAIR[pr]].rearrange("p h s -> p (h s)"),
                                 start=True, stop=True).then_inc(p_s, 1)

            def transposed_heads(l, gi):
                name = GROUPS[gi]
                qo, ko, _, nq, nk = SEG[name]
                pe.wait_ge(v_qk, 3 * l + gi + 1)
                for b, bk in enumerate(Q_BANKS[gi]):
                    for pr in range(2):
                        for t in range(TT):
                            o0 = qo + (2 * b + pr) * P
                            c = (2 * pr + t) * P
                            last = nc.tensor.transpose(bank[bk][:, c:c + P], proj[:, t, o0:o0 + P], ident[:])
                    last.then_inc(p_qk, 1)
                if gi == 1:
                    pe.wait_ge(v_keys, 3 * l + 1)
                for pr in range(2):
                    for t in range(TT):
                        c = (2 * pr + t) * P
                        src = proj[:, t, ko + pr * P:ko + pr * P + P] if name != "C" else \
                            hn[:, t, 640 + pr * P:640 + pr * P + P]
                        last = nc.tensor.transpose(bank[K_BANK[gi]][:, c:c + P], src, ident[:])
                last.then_inc(p_qk, 1)

            def mixers(l, e0):
                pe.wait_ge(d_rel, 80 * (l + 1))
                pe.wait_ge(v_x, 3 * l + 1)
                for h in range(4):
                    nc.tensor.matmul(bank[4 + h][:, 0:7 * GRID], flip, relrev[:, h].rearrange("p r c -> p (r c)"),
                                     start=True, stop=True).then_inc(p_flip, 1)
                transposed_rows(l)
                pe.wait_ge(v_hT, 6 * l + 2)
                pe.wait_ge(a_hT, 6 * l + 2)
                for gi, name in enumerate(GROUPS):
                    for i in range(4):
                        if gi == 2 and i == 3:
                            transposed_heads(l, 1)
                            pe.wait_ge(a_q, 4 * l + 2)
                            pe.wait_ge(v_keys, 3 * l + 1)
                            scores(l, 0)
                            scores(l, 1)
                        u, t, c0 = 4 * gi + i, i // 2, i % 2 * HALF_SEG
                        if t == 0:
                            pe.wait_ge(landed[gi][i], 16 * (l * USES + 1 + e0))
                        if gi == 0:
                            pe.wait_ge(v_rel, 4 * l + u + 1)
                        else:
                            pe.wait_ge((v_proj, a_proj)[u % 2], 6 * l + (u - 4) // 2 + 1)
                        for k in range(KD):
                            last = nc.tensor.matmul(bank[4 + i][:, 0:HALF_SEG], hT[:, k, t * P:t * P + P],
                                                    slot8[gi][:, k, c0:c0 + HALF_SEG], start=(k == 0), stop=(k == KD - 1))
                        last.then_inc(p_proj, 1)
                    if gi == 1:
                        transposed_heads(l, 0)
                pe.wait_ge(a_q, 4 * l + 3)
                pe.wait_ge(v_keys, 3 * l + 2)
                for step in range(2, N_UNITS + 3):
                    if step == N_UNITS // 2 - 2:
                        transposed_heads(l, 2)
                    elif step == N_UNITS // 2:
                        pe.wait_ge(a_q, 4 * l + 4)
                        pe.wait_ge(v_keys, 3 * l + 3)
                    if step < N_UNITS:
                        scores(l, step)
                    u = step - 2
                    if 0 <= u < N_UNITS:
                        pe.wait_ge(a_exp, N_UNITS * l + u + 1)
                        if u >= 1:
                            pe.wait_ge(a_pt, N_UNITS * l + u)
                        for c in range(4):
                            last = nc.tensor.transpose(bank[3][:, c * P:c * P + P],
                                                       prob[u % 3][:, c * P:c * P + P], ident[:])
                        last.then_inc(p_pt, 1)
                    u = step - 3
                    if u >= 0:
                        pe.wait_ge(a_pt, N_UNITS * l + u + 1)
                        for h in range(2):
                            head, t = 2 * UNITS[u][0] + h, UNITS[u][1]
                            if head < 8:
                                vcol = SEG["AB"[head // 4]][2] + head % 4 * HD
                            else:
                                vcol = SEG["C"][2] + (head - 8) // 4 * HD
                            for kt in range(TT):
                                last = nc.tensor.matmul(
                                    bank[4 + 2 * t + head // 8][:, head % 8 * HD:head % 8 * HD + HD],
                                    probT[u % 2][:, (2 * h + kt) * P:(2 * h + kt) * P + P],
                                    proj[:, kt, vcol:vcol + HD], start=(kt == 0), stop=(kt == 1))
                        last.then_inc(p_pv, 1)
                def out_product(n):
                    t, half = n // 2, n % 2
                    for k in range(KD):
                        last = nc.tensor.matmul(bank[n][:, :], hT[:, k, t * P:t * P + P],
                                                slot8[3][:, k, half * 512:half * 512 + 512],
                                                start=(k == 0), stop=(k == KD - 1))
                    last.then_inc(p_out, 1)

                def logits(t):
                    for k in range(KD):
                        last = nc.tensor.matmul(bank[4][:, t * 36:t * 36 + 36], hT[:, k, t * P:t * P + P],
                                                w_route[:, k, :], start=(k == 0), stop=(k == KD - 1))
                    last.then_inc(p_logit, 1)

                transposed_tile(l, 0)
                tile_ready(l, 0)
                for half in range(2):
                    pe.wait_ge(landed[3][half], 16 * (l * USES + 1))
                out_product(0)
                transposed_tile(l, 1)
                out_product(1)
                tile_ready(l, 1)
                out_product(2)
                transposed_tile(l, 2)
                out_product(3)
                tile_ready(l, 2)
                pe.wait_ge(d_small, 80 * (l + 1))
                logits(0)
                transposed_tile(l, 3)
                tile_ready(l, 3)
                logits(1)
                pe.wait_ge(v_chosen, l + 1)
                pe.wait_ge(d_const, 96)
                for c, terms in enumerate((((tri, 0),), ((tri, 1), (ones, 0)), ((ones, 0), (ones, 1)))):
                    for n, (w, t) in enumerate(terms):
                        last = nc.tensor.matmul(bank[5][:, c * NE:c * NE + NE], w[:], chosen[:, t, :],
                                                start=(n == 0), stop=(n == len(terms) - 1))
                last.then_inc(p_rank, 1)
                pe.wait_ge(g_part, l + 1)

            def gather(gq, pair=None, ps=None):
                pe.wait_ge(v_pick, gq + (AHEAD + 1))
                pe.wait_ge(v_xg, gq + AHEAD)
                pe.wait_ge(a_xg, gq + AHEAD)
                for k in range(KD):
                    n = 0
                    for t in range(TT):
                        for part in range(3):
                            last = nc.tensor.matmul(bank[k // 4][:, k % 4 * P:k % 4 * P + P], xpart[:, part, t, k, :],
                                                    pick[:, t, :], start=(n == 0), stop=(n == 5))
                            n += 1
                    if k % 4 == 3:
                        last.then_inc(p_gather, 1)

            def item(q, gq, slots, rounds, pair, has_next):
                def by_expert(banks, weights, k_count, lhs, j, done):
                    s = slots[j]
                    for half in range(2):
                        pe.wait_ge(landed[s][half], rounds[j] * 16 + 16)
                        for n, b in enumerate(banks):
                            for k in range(half * k_count // 2, (half + 1) * k_count // 2):
                                for e in range(2):
                                    last = nc.tensor.matmul(bank[b][e * CAP:e * CAP + CAP, :], lhs[:, k, e * CAP:e * CAP + CAP],
                                                            weights[s][:, e, k, n * 512:n * 512 + 512],
                                                            start=(k == 0), stop=(k == k_count - 1))
                            if half or done is p_gate:
                                last.then_inc(done, 1)

                pe.wait_ge(v_xg, gq + (AHEAD + 1))
                pe.wait_ge(a_xg, gq + (AHEAD + 1))
                pe.wait_ge(v_back[0], q + AHEAD)
                by_expert((2,), slot_up, KD, xg, 0, p_gate)
                pe.wait_ge(v_back[3], q + AHEAD)
                pe.wait_ge(v_pickw, gq + (AHEAD + 1))
                for t in range(TT):
                    last = nc.tensor.transpose(bank[5][:, t * P:t * P + P], pickw[:, t, :], ident[:])
                last.then_inc(p_pickT, 1)
                pe.wait_ge(v_back[1], q + AHEAD)
                by_expert((3,), slot_up, KD, xg, 1, p_up)
                if has_next:
                    gather(gq + 1)
                pe.wait_ge(v_hid, q + (AHEAD + 1))
                pe.wait_ge(v_back[2], q + AHEAD)
                hidc = hid.rearrange("p (f c) -> p c f", c=KE)
                for c in range(KE):
                    last = nc.tensor.transpose(bank[4][:, c * P:c * P + P], hidc[:, c, :], ident[:])
                last.then_inc(p_hidT, 1)
                pe.wait_ge(a_hidT, q + (AHEAD + 1))
                pe.wait_ge(a_y, q + AHEAD)
                pe.wait_ge(v_y, q + AHEAD)
                by_expert((6, 7), slot_dn, KE, hidT, 2, p_down)
                pe.wait_ge(a_pickT, q + (AHEAD + 1))
                pe.wait_ge(a_y, q + (AHEAD + 1))
                for n, (t, half) in enumerate(BACK):
                    if n == 2:
                        pe.wait_ge(v_y, q + (AHEAD + 1))
                    last = nc.tensor.matmul(bank[2 + n][:, :], pickT[:, t, :], y[:, half * 512:half * 512 + 512],
                                            start=True, stop=True)
                    last.then_inc(p_back, 1)

            run_layers(pe, extra, mixers, gather, item, seen[1])

        @block.scalar
        def _(act):
            extra = act.alloc_register("act_extra")
            act.reg_mov(extra, 0)
            for s in (a_silu, a_pickT, a_xg, a_hidT, a_y):
                act.sem_inc(s, AHEAD)

            def hT_tile(l, m):
                t, b0 = TILE_STAGES[m]
                act.wait_ge(p_tr, 12 * l + 6 + 2 * m)
                nc.scalar.copy(hT[:, 4:8, t * P:t * P + P], bank[b0 + 1][:, :].rearrange("p (k s) -> p k s", k=4)).then_inc(a_hT, 1)

            def mean_squares(t, c):
                return nc.scalar.activation(hn[:, t, :], x[:, t, :], ACT.Square, scale=D ** -0.5, accum_out=ms[:, c:c + 1])

            def exponentials(l, u):
                act.wait_ge(v_soft, N_UNITS * l + u + 1)
                if u >= 3:
                    act.wait_ge(p_pt, N_UNITS * l + u - 2)
                pr, t = UNITS[u]
                for h in range(2):
                    dst = prob[u % 3][:, h * SEQ:h * SEQ + SEQ]
                    src = dst if pr < 4 else bank[u % 3][:, h * SEQ:h * SEQ + SEQ]
                    last = nc.scalar.activation(dst, src, ACT.Exp, bias=nmax[:, u % 3, h:h + 1],
                                                scale=1.0 if pr < 4 else SCALE,
                                                accum_out=den[:, t, 2 * pr + h:2 * pr + h + 1])
                last.then_inc(a_exp, 1)

            def mixer_squares(l, t):
                act.wait_ge(v_o, 4 * l + 2 * t + 2)
                for n, (c0, w) in enumerate(((0, 256), (256, 256), (512, 512))):
                    last = nc.scalar.activation(squares[c0 // 512][:, c0 % 512:c0 % 512 + w], hn[:, t, c0:c0 + w], ACT.Square,
                                                scale=w ** -0.5, accum_out=ms[:, 3 * t + n:3 * t + n + 1])
                last.then_inc(a_ss, 1)

            def copy_queries(l, gi):
                for b, (bk, n) in enumerate(zip(Q_BANKS[gi], Q_DONE[gi])):
                    act.wait_ge(p_qk, 7 * l + n)
                    dst = q_c[:, 2 * b:2 * b + 2, :] if gi == 0 else hT[:, 2 * gi - 2:2 * gi, :]
                    nc.scalar.copy(dst.rearrange("p k s -> p (k s)"), bank[bk][:, :]).then_inc(a_q, 1)

            def mixers(l, e0):
                act.wait_ge(v_x, 3 * l + 1)
                mean_squares(0, 0)
                mean_squares(1, 1).then_inc(a_ss, 1)
                for j in (1, 3):
                    act.wait_ge(p_tr, 12 * l + j + 1)
                    nc.scalar.copy(hT[:, 2 * j:2 * j + 2, :].rearrange("p k s -> p (k s)"), bank[j][:, :]).then_inc(a_hT, 1)
                for gi, name in enumerate(GROUPS):
                    qo, _, vo, _, _ = SEG[name]
                    for t in range(TT):
                        if gi == 2 and t == 1:
                            exponentials(l, 0)
                            exponentials(l, 1)
                        act.wait_ge(p_proj, 12 * l + 4 * gi + 2 * t + 2)
                        nc.scalar.copy(proj[:, t, qo + HALF_SEG:qo + SEG_COLS], bank[5 + 2 * t][:, 0:HALF_SEG]).then_inc(a_proj, 1)
                        act.wait_ge(v_proj, 6 * l + 2 * gi + t + 1)
                        act.wait_ge(a_proj, 6 * l + 2 * gi + t + 1)
                        if gi == 1 and t == 0:
                            act.wait_ge(v_qk, 3 * l + 1)
                        if gi == 2 and t == 0:
                            act.wait_ge(v_ssh, 6 * l + 4)
                        nc.scalar.activation(hn[:, t, 0:vo - qo], proj[:, t, qo:vo], ACT.Square, scale=HD ** -0.5).then_inc(a_sq, 1)
                    if gi == 1:
                        copy_queries(l, 0)
                copy_queries(l, 1)
                for step in range(2, N_UNITS + 2):
                    u = step - 2
                    act.wait_ge(p_pt, N_UNITS * l + u + 1)
                    if u >= 2:
                        act.wait_ge(p_pv, N_UNITS * l + u - 1)
                    nc.scalar.copy(probT[u % 2], bank[3][:, :]).then_inc(a_pt, 1)
                    if step < N_UNITS:
                        exponentials(l, step)
                    if step == N_UNITS // 2 - 2:
                        copy_queries(l, 2)
                    if step == N_UNITS - 1:
                        mixer_squares(l, 0)
                hT_tile(l, 0)
                mixer_squares(l, 1)
                hT_tile(l, 1)
                for t in range(TT):
                    act.wait_ge(v_x, 3 * l + 2 + t)
                    mean_squares(t, 6 + t).then_inc(a_ss, 1)
                    hT_tile(l, 2 + t)
                    act.wait_ge(v_hn, 6 * l + 5 + t)
                    nc.scalar.copy(xpart[:, 0, t], hn_kc[:, t]).then_inc(a_part, 1)
                act.wait_ge(v_router, 2 * l + 1)
                nc.scalar.activation(rb[:, :, 0:NG], ra[:, :, 0:NG], ACT.Exp).then_inc(a_rexp, 1)
                act.wait_ge(v_part, l + 1)
                for t in range(TT):
                    last = nc.scalar.copy(xpart[:, 1, t], hn_kc[:, t])
                last.then_inc(a_part, 1)
                act.wait_ge(v_router, 2 * l + 2)
                nc.scalar.activation(col[:, 4, :], col[:, 3, :], ACT.Exp).then_inc(a_rexp, 1)

            def gathered(gq, pair=None, ps=None):
                act.wait_ge(p_gather, gq * 2 + (AHEAD + 2))
                nc.scalar.copy(xg[:, 4:8, :].rearrange("p k s -> p (k s)"), bank[1][:, :]).then_inc(a_xg, 1)

            def item(q, gq, slots, rounds, pair, has_next):
                act.wait_ge(p_pickT, q + (AHEAD + 1))
                act.wait_ge(p_back, q * 4 + AHEAD)
                nc.scalar.copy(pickT.rearrange("p t s -> p (t s)"), bank[5][:, 0:2 * P]).then_inc(a_pickT, 1)
                act.wait_ge(p_gate, q * 2 + (AHEAD + 2))
                act.wait_ge(p_hidT, q + AHEAD)
                nc.scalar.activation(hid, bank[2][:, :], ACT.Silu).then_inc(a_silu, 1)
                if has_next:
                    act.wait_ge(p_up, q + (AHEAD + 1))
                    gathered(gq + 1)
                act.wait_ge(p_hidT, q + (AHEAD + 1))
                act.wait_ge(p_down, q * 2 + AHEAD)
                nc.scalar.copy(hidT.rearrange("p c s -> p (c s)"), bank[4][:, :]).then_inc(a_hidT, 1)
                act.wait_ge(p_down, q * 2 + (AHEAD + 1))
                nc.scalar.copy(y[:, 0:512], bank[6][:, :]).then_inc(a_y, 1)

            run_layers(act, extra, mixers, gathered, item, seen[2])

        @block.vector
        def _(dve):
            extra = dve.alloc_register("dve_extra")
            dve.reg_mov(extra, 0)
            for s in (v_pick, v_pickw, v_xg, v_hid, v_y, v_istep, *v_back):
                dve.sem_inc(s, AHEAD)
            steps = [0, 0]
            tt, ts, stt = nc.vector.tensor_tensor, nc.vector.tensor_scalar, nc.vector.scalar_tensor_tensor

            def link(ins):
                steps[0] += 1
                ins.then_inc(v_step, 1)
                dve.wait_ge(v_step, steps[1] * V_STEPS + steps[0])

            def wide(ap, n):
                return ap.unsqueeze(len(ap.shape)).broadcast_to(list(ap.shape) + [n])

            def over(ap, axis, n):
                shape = list(ap.shape)
                shape.insert(axis, n)
                return ap.unsqueeze(axis).broadcast_to(shape)

            def hT_tile(l, m):
                t, b0 = TILE_STAGES[m]
                dve.wait_ge(p_tr, 12 * l + 5 + 2 * m)
                nc.vector.tensor_copy(hT[:, 0:4, t * P:t * P + P], bank[b0][:, :].rearrange("p (k s) -> p k s", k=4)).then_inc(v_hT, 1)

            def norm_row(t, c):
                stt(hn[:, t, :], x[:, t, :], rstd[:, c:c + 1], gain[:], ALU.mult, ALU.mult).then_inc(v_hn, 1)

            def mixed(l, t):
                dve.wait_ge(a_exp, N_UNITS * l + (TILE0_UNITS, N_UNITS)[t])
                link(nc.vector.reciprocal(rden[:, t], den[:, t]))
                dve.wait_ge(p_pv, N_UNITS * l + (TILE0_UNITS, N_UNITS)[t])
                for b in range(2):
                    tt(hn[:, t, b * 512:b * 512 + 512].rearrange("p (h d) -> p h d", d=HD),
                       bank[4 + 2 * t + b][:, :].rearrange("p (h d) -> p h d", d=HD),
                       wide(rden[:, t, 8 * b:8 * b + 8], HD), ALU.mult).then_inc(v_o, 1)

            def mixed_norm(l, t):
                dve.wait_ge(v_o, 4 * l + 2 * t + 2)
                dve.wait_ge(g_rstd, 8 * l + 5 + t)
                dve.wait_ge(d_gain, 32 * l + 16)
                for n, (c0, w) in enumerate(((0, 256), (256, 256), (512, 512))):
                    last = stt(hn[:, t, c0:c0 + w], hn[:, t, c0:c0 + w], rstd[:, 3 * t + n:3 * t + n + 1],
                               gain[:, c0:c0 + w], ALU.mult, ALU.mult)
                last.then_inc(v_hn, 1)

            def copy_proj(l, gi, t):
                qo = SEG[GROUPS[gi]][0]
                dve.wait_ge(p_proj, 12 * l + 4 * gi + 2 * t + 1)
                nc.vector.tensor_copy(proj[:, t, qo:qo + HALF_SEG], bank[4 + 2 * t][:, 0:HALF_SEG]).then_inc(v_proj, 1)

            def sum_squares(l, gi):
                qo, _, vo, nq, nk = SEG[GROUPS[gi]]
                h0 = HEAD0[GROUPS[gi]]
                for t in range(TT):
                    dve.wait_ge(a_sq, 6 * l + 2 * gi + t + 1)
                    nc.vector.tensor_reduce(msh[:, t, h0:h0 + nq + nk], hn[:, t, 0:vo - qo].rearrange("p (h d) -> p h d", d=HD),
                                            AX_X, ALU.add).then_inc(v_ssh, 1)

            def normalise(l, gi):
                name = GROUPS[gi]
                qo, ko, vo, nq, nk = SEG[name]
                h0 = HEAD0[name]
                dve.wait_ge(a_proj, 6 * l + 2 * gi + 2)
                dve.wait_ge(v_proj, 6 * l + 2 * gi + 2)
                dve.wait_ge(g_rstd, 8 * l + 2 + gi)
                dve.wait_ge(d_small, 80 * (l + 1))
                heads = proj[:, :, qo:vo].rearrange("p t (h d) -> p t h d", d=HD)
                link(tt(heads, heads, wide(rsh[:, :, h0:h0 + nq + nk], HD), ALU.mult))
                qh, kh = heads[:, :, 0:nq, :], heads[:, :, nq:, :]
                which = "ABC".index(name)
                gq = over(over(qkg[:, 2 * which, :], 1, nq), 1, TT)
                gk = over(over(qkg[:, 2 * which + 1, :], 1, nk), 1, TT)
                tt(qh, qh, gq, ALU.mult)
                if name != "C":
                    tt(kh, kh, gk, ALU.mult).then_inc(v_qk, 1)
                    return
                link(tt(kh, kh, gk, ALU.mult))
                dve.wait_ge(d_const, 96)
                part = hn[:, :, 0:(nq + nk) * HD].rearrange("p t (h d) -> p t h d", d=HD)
                for t in range(TT):
                    src = heads[:, t].rearrange("p h (a b f) -> p h a b f", a=2, b=2)
                    dst = part[:, t].rearrange("p h (a b f) -> p h a b f", a=2, b=2)
                    sin = rope[:, t, 1, :].rearrange("p (a b f) -> p a b f", a=2, b=2)
                    for b in range(2):
                        last = tt(dst[:, :, :, b, :], src[:, :, :, 1 - b, :], over(sin[:, :, b, :], 1, nq + nk), ALU.mult)
                link(last)
                for t in range(TT):
                    last = tt(heads[:, t], heads[:, t], over(rope[:, t, 0, :], 1, nq + nk), ALU.mult)
                link(last)
                for t in range(TT):
                    tt(hn[:, t, 640:896].rearrange("p (k c d) -> p k c d", k=nk, c=2),
                       over(heads[:, t, nq:, :], 2, 2), over(part[:, t, nq:, :], 2, 2), ALU.add)
                tt(qh, qh, part[:, :, 0:nq, :], ALU.add).then_inc(v_qk, 1)

            def copy_keys(l, gi):
                j0 = (4, 0, 2)[gi]
                dve.wait_ge(g_keys0, l + 1)
                dve.wait_ge(p_qk, 7 * l + K_DONE[gi])
                for h in range(2):
                    src = bank[K_BANK[gi]][64 * h:64 * h + 64, :].rearrange("p (j s) -> p j s", j=2)
                    last = nc.vector.tensor_copy(keys[64 * h:64 * h + 64, j0:j0 + 2, h, :], src)
                last.then_inc(v_keys, 1)

            def mixers(l, e0):
                steps[0], steps[1] = 0, l
                dve.wait_ge(d_x, 16)
                for n in range(4):
                    dve.wait_ge(v_back[n], l * EPAIRS + e0 + AHEAD)
                nc.vector.memset(mark[:], 0.0).then_inc(v_x, 1)
                dve.wait_ge(g_rstd, 8 * l + 1)
                dve.wait_ge(d_gain1, 16 * l + 16)
                norm_row(0, 0)
                norm_row(1, 1)
                for j in (0, 2):
                    dve.wait_ge(p_tr, 12 * l + j + 1)
                    nc.vector.tensor_copy(hT[:, 2 * j:2 * j + 2, :].rearrange("p k s -> p (k s)"), bank[j][:, :]).then_inc(v_hT, 1)
                dve.wait_ge(d_first, 32)
                for h in range(4):
                    dve.wait_ge(p_flip, 4 * l + h + 1)
                    tt(rel[:, h], bank[4 + h][:, 0:7 * GRID].rearrange("p (r c) -> p r c", c=GRID),
                       over(colmask[:], 1, 7), ALU.min).then_inc(v_rel, 1)
                for gi in range(3):
                    copy_proj(l, gi, 0)
                    if gi:
                        normalise(l, gi - 1)
                    if gi == 2:
                        copy_keys(l, 0)
                    copy_proj(l, gi, 1)
                    if gi < 2:
                        sum_squares(l, gi)
                copy_keys(l, 1)
                dve.wait_ge(v_rel, 4 * l + 4)
                for u in range(N_UNITS):
                    if u == 2:
                        sum_squares(l, 2)
                    if u == 3:
                        normalise(l, 2)
                    if u == N_UNITS // 2 - 2:
                        copy_keys(l, 2)
                    if u == N_UNITS - 1:
                        mixed(l, 0)
                    pr, t = UNITS[u]
                    dve.wait_ge(p_s, N_UNITS * l + u + 1)
                    if u >= 3:
                        dve.wait_ge(p_pt, N_UNITS * l + u - 2)
                    sc = bank[u % 3][:, :].rearrange("p (h s) -> p h s", h=2)
                    pb = prob[u % 3].rearrange("p (h s) -> p h s", h=2)
                    if pr < 2:
                        for rr in range(2):
                            r = 2 * t + rr
                            rows = slice(64 * rr, 64 * rr + 64)
                            last = stt(pb[rows], sc[rows], SCALE,
                                       rel[rows, 2 * pr:2 * pr + 2, 3 - r:7 - r, :].rearrange("p h r c -> p h (r c)"),
                                       ALU.mult, ALU.add)
                        link(last)
                        nc.vector.tensor_reduce(nmax[:, u % 3, 0:2], pb, AX_X, ALU.max, negate=True).then_inc(v_soft, 1)
                    elif pr < 4:
                        c0 = (1 - t) * P
                        link(stt(pb, sc, SCALE, dil[:, 2 * pr - 4:2 * pr - 2, c0:c0 + SEQ], ALU.mult, ALU.add))
                        nc.vector.tensor_reduce(nmax[:, u % 3, 0:2], pb, AX_X, ALU.max, negate=True).then_inc(v_soft, 1)
                    else:
                        link(nc.vector.tensor_reduce(nmax[:, u % 3, 2:4], sc, AX_X, ALU.max, negate=True))
                        ts(nmax[:, u % 3, 0:2], nmax[:, u % 3, 2:4], SCALE, None, ALU.mult).then_inc(v_soft, 1)
                mixed_norm(l, 0)
                mixed(l, 1)
                hT_tile(l, 0)
                mixed_norm(l, 1)
                hT_tile(l, 1)
                for t in range(TT):
                    for half in range(2):
                        n = 2 * t + half
                        dve.wait_ge(p_out, 4 * l + n + 1)
                        xs = x[:, t, half * 512:half * 512 + 512]
                        last = tt(xs, xs, bank[n][:, :], ALU.add)
                    last.then_inc(v_x, 1)
                    dve.wait_ge(v_x, 3 * l + 2 + t)
                    dve.wait_ge(g_rstd, 8 * l + 7 + t)
                    dve.wait_ge(d_gain, 32 * l + 32)
                    norm_row(t, 6 + t)
                    hT_tile(l, 2 + t)
                dve.wait_ge(a_part, 3 * l + 2)
                dve.wait_ge(p_tr, 12 * l + 12)
                for t in range(TT):
                    last = tt(hn_kc[:, t], hn_kc[:, t], xpart[:, 0, t], ALU.subtract)
                last.then_inc(v_part, 1)
                dve.wait_ge(p_logit, 2 * l + 2)
                dve.wait_ge(d_small, 80 * (l + 1))
                link(tt(lg[:], bank[4][:, 0:72].rearrange("p (t n) -> p t n", t=TT), over(b_route[:], 1, TT), ALU.add))
                gl, el = lg[:, :, 0:NG], lg[:, :, NG:36]
                link(nc.vector.tensor_reduce(col[:, 0, :], gl, AX_X, ALU.max))
                tt(ra[:, :, 0:NG], gl, wide(col[:, 0, :], NG), ALU.subtract).then_inc(v_router, 1)
                dve.wait_ge(v_router, 2 * l + 1)

                def first_of_max(dst, score, diff, n, r0, c):
                    link(stt(score, diff, 0.0, over(rev[:, r0:r0 + n], 1, TT), ALU.is_equal, ALU.mult))
                    link(nc.vector.tensor_reduce(col[:, c, :], score, AX_X, ALU.max))
                    link(tt(dst, score, wide(col[:, c, :], n), ALU.is_equal))

                first_of_max(ra[:, :, 8:12], ra[:, :, 4:8], ra[:, :, 0:NG], NG, 0, 1)
                link(ts(ra[:, :, 12:16], ra[:, :, 8:12], BIG, -BIG, ALU.mult, ALU.add))
                link(tt(el.rearrange("p t (g e) -> p t g e", g=NG), el.rearrange("p t (g e) -> p t g e", g=NG),
                        wide(ra[:, :, 12:16], EPG), ALU.add))
                link(nc.vector.tensor_reduce(col[:, 1, :], el, AX_X, ALU.max))
                dve.wait_ge(a_rexp, 2 * l + 1)
                link(nc.vector.tensor_reduce(col[:, 5, :], rb[:, :, 0:NG], AX_X, ALU.add))
                link(tt(ra[:, :, 4:36], el, wide(col[:, 1, :], NE), ALU.subtract))
                first_of_max(oh1[:], rb[:, :, 4:36], ra[:, :, 4:36], NE, 4, 6)
                link(stt(el, oh1[:], -BIG, el, ALU.mult, ALU.add))
                link(nc.vector.tensor_reduce(col[:, 2, :], el, AX_X, ALU.max))
                tt(col[:, 3, :], col[:, 2, :], col[:, 1, :], ALU.subtract).then_inc(v_router, 1)
                link(tt(ra[:, :, 4:36], el, wide(col[:, 2, :], NE), ALU.subtract))
                first_of_max(oh2[:], rb[:, :, 4:36], ra[:, :, 4:36], NE, 4, 6)
                tt(chosen[:], oh1[:], oh2[:], ALU.add).then_inc(v_chosen, 1)
                nc.vector.memset(rg[:, :, NE:], -1.0)
                dve.wait_ge(p_rank, l + 1)
                dve.wait_ge(v_chosen, l + 1)
                link(stt(rb[:, :, 0:NE], bank[5][:, 0:2 * NE].rearrange("p (t n) -> p t n", t=TT), 1.0, chosen[:],
                         ALU.add, ALU.mult))
                link(ts(rg[:, 0:TT, 0:NE], rb[:, :, 0:NE], -1.0, None, ALU.add))
                counts = bank[5][0:1, 2 * NE:3 * NE].rearrange("p (j e) -> p j e", e=2)
                link(nc.vector.tensor_reduce(pairmax[:], counts, AX_X, ALU.max))

            def gates(l):
                link(nc.vector.reciprocal(col[:, 7, :], col[:, 5, :]))
                dve.wait_ge(a_rexp, 2 * l + 2)
                link(ts(col[:, 8, :], col[:, 4, :], 1.0, None, ALU.add))
                link(nc.vector.reciprocal(col[:, 9, :], col[:, 8, :]))
                link(tt(col[:, 10, :], col[:, 9, :], col[:, 7, :], ALU.mult))
                link(tt(col[:, 11, :], col[:, 10, :], col[:, 4, :], ALU.mult))
                tt(oh1[:], oh1[:], wide(col[:, 10, :], NE), ALU.mult)
                link(tt(oh2[:], oh2[:], wide(col[:, 11, :], NE), ALU.mult))
                link(tt(rg[:, TT:2 * TT, 0:NE], oh1[:], oh2[:], ALU.add))

            def list_again():
                n = (PASSES - 1) * EPAIRS
                rank, score = (m[0:1].rearrange("p t h -> p (t h)")[:, 0:n] for m in (msh, rsh))
                top, idx, run, nonzero = (den[0:1].rearrange("p t h -> p (t h)")[:, i * AGAIN:i * AGAIN + AGAIN] for i in range(4))
                link(ts(rank, iota[0:1, 0:n], -1.0, float(n), ALU.mult, ALU.add))
                for ps in range(PASSES - 1):
                    part = slice(ps * EPAIRS, ps * EPAIRS + EPAIRS)
                    last = stt(score[:, part], pairmax[:], float(CAP * (ps + 1)), rank[:, part], ALU.is_gt, ALU.mult)
                link(last)
                dve.sem_inc(seen[3], 1)
                link(nc.vector.max(top, score))
                ts(nonzero, top, 0.0, None, ALU.is_gt)
                link(ts(idx, top, -1.0, float(n), ALU.mult, ALU.add))
                link(ts(run, idx, EPAIRS - 0.5, None, ALU.is_gt))
                link(stt(run, idx, 2 * EPAIRS - 0.5, run, ALU.is_gt, ALU.add))
                stt(again[:, 0:AGAIN], run, -float(EPAIRS), idx, ALU.mult, ALU.add)
                nc.vector.tensor_copy(again[:, AGAIN:2 * AGAIN], run)
                link(nc.vector.tensor_reduce(rden[0:1, 0, 0:1], nonzero, AX_X, ALU.add))
                nc.vector.tensor_copy(again[:, 2 * AGAIN:2 * AGAIN + 1], rden[0:1, 0, 0:1]).then_inc(v_flags, 1)
                assert steps[0] == V_STEPS, steps

            def picks(gq, pair, ps, between=None):
                columns = rg[:, :, bass.ds(pair * 2, 2)] if not isinstance(pair, int) else rg[:, :, 2 * pair:2 * pair + 2]
                nc.vector.tensor_copy(rgc[:, 0:TT], columns[:, 0:TT]).then_inc(v_istep, 1)
                dve.wait_ge(v_istep, gq * 2 + (AHEAD + 1))
                places = iota[:, 0:CAP] if ps is None else iota[:, bass.ds(ps * CAP + CAP, CAP)]
                hot = pick.rearrange("p t (e s) -> p (t e) s", e=2)
                tt(hot, over(places, 1, 2 * TT), wide(rgc[:, 0:TT, :].rearrange("p t e -> p (t e)"), CAP),
                   ALU.is_equal).then_inc(v_pick, 1)
                if between:
                    between()
                nc.vector.tensor_copy(rgc[:, TT:], columns[:, TT:]).then_inc(v_istep, 1)
                dve.wait_ge(v_istep, gq * 2 + (AHEAD + 2))
                dve.wait_ge(v_pick, gq + (AHEAD + 1))
                tt(pickw.rearrange("p t (e s) -> p (t e) s", e=2), hot,
                   wide(rgc[:, TT:2 * TT, :].rearrange("p t e -> p (t e)"), CAP), ALU.mult).then_inc(v_pickw, 1)

            def copy_gathered(gq):
                dve.wait_ge(p_gather, gq * 2 + (AHEAD + 1))
                nc.vector.tensor_copy(xg[:, 0:4, :].rearrange("p k s -> p (k s)"), bank[0][:, :]).then_inc(v_xg, 1)

            def first(gq, pair, ps):
                picks(gq, pair, ps, (lambda: gates(steps[1])) if ps is None else None)
                if ps is None:
                    list_again()
                copy_gathered(gq)

            def item(q, gq, slots, rounds, pair, has_next):
                if has_next:
                    dve.wait_ge(p_pickT, q + (AHEAD + 1))
                    picks(gq + 1, pair + 1, None)
                dve.wait_ge(a_silu, q + (AHEAD + 1))
                dve.wait_ge(p_up, q + (AHEAD + 1))
                tt(hid, hid, bank[3][:, :], ALU.mult).then_inc(v_hid, 1)
                if has_next:
                    copy_gathered(gq + 1)
                dve.wait_ge(p_down, q * 2 + (AHEAD + 2))
                dve.wait_ge(p_back, q * 4 + AHEAD)
                nc.vector.tensor_copy(y[:, 512:1024], bank[7][:, :]).then_inc(v_y, 1)
                for n, (t, half) in enumerate(BACK):
                    dve.wait_ge(p_back, q * 4 + (AHEAD + n + 1))
                    dve.wait_ge(v_back[n], q + AHEAD)
                    xs = x[:, t, half * 512:half * 512 + 512]
                    tt(xs, xs, bank[2 + n][:, :], ALU.add).then_inc(v_back[n], 1)

            run_layers(dve, extra, mixers, first, item, seen[3])
            e = dve.snap(extra, min_val=0, max_val=96)
            for n in range(4):
                dve.wait_ge(v_back[n], e + (LAYERS * EPAIRS + AHEAD))
            nc.vector.memset(mark[:], 0.0).then_inc(v_x, 1)


_INS = ["x", "norm1_g", "w_in", "qk_norm_g", "na_rpb", "mix_norm_g", "w_out", "norm2_g", "w_router_group",
        "b_router_group", "w_router_expert", "b_router_expert", "w_gate", "w_up", "w_down"]


def shape_constants():
    t = np.arange(SEQ)
    nf = HD // 4
    inv = (10000.0 ** (-np.arange(nf, dtype=np.float32) / nf)).astype(np.float32)
    ang = np.stack([(t // GRID).astype(np.float32)[:, None] * inv, (t % GRID).astype(np.float32)[:, None] * inv], 1)
    cos = np.repeat(np.cos(ang)[:, :, None, :], 2, axis=2).reshape(SEQ, HD)
    sin = np.stack([-np.sin(ang), np.sin(ang)], axis=2).reshape(SEQ, HD)
    rope = np.stack([cos, sin], 1).reshape(TT, P, 2, HD).transpose(1, 0, 2, 3)
    c = np.arange(P)[:, None] % GRID
    start = np.clip(c - 8, 0, GRID - 16)
    kc = np.arange(GRID)[None, :]
    colmask = np.where((kc >= start) & (kc < start + 16), 3e38, -BIG)
    dist = np.abs(np.arange(P)[:, None] - (np.arange(3 * P)[None, :] - P))
    count = (dist <= 64).astype(int) + ((dist % 4 == 0) & (dist <= 256)) + ((dist % 16 == 0) & (dist <= 1024))
    slope = 2.0 ** (-8.0 * np.arange(1, 5) / 4)
    base = np.where(count > 0, np.log(np.maximum(count, 1)), -BIG)
    dil = base[:, None, :] - slope[None, :, None] * dist[:, None, :] * (count > 0)[:, None, :]
    return {
        "c_rope": np.ascontiguousarray(rope, np.float32), "c_colmask": colmask.astype(np.float32),
        "c_flip": np.tile(np.eye(GRID, dtype=np.float32)[::-1], (1, 2)),
        "c_ident": np.eye(P, dtype=np.float32), "c_dil": dil.astype(np.float32),
        "c_tri": np.triu(np.ones((P, P)), 1), "c_ones": np.ones((P, P)),
        "c_iota": np.tile(np.arange(SEQ, dtype=np.float32), (P, 1)),
        "c_rev": np.tile(np.concatenate([np.arange(4, 0, -1), np.arange(32, 0, -1)]).astype(np.float32), (P, 1)),
    }


def kernel(**inputs):
    import ml_dtypes
    import concourse.bacc as _bacc
    from concourse import mybir as _mybir
    from concourse.bass_utils import run_bass_kernel_spmd as _run

    nc = _bacc.Bacc("TRN2", target_bir_lowering=False, num_devices=1)
    arrays, aps = {}, {}
    consts = shape_constants()
    for name in ("c_tri", "c_ones"):
        consts[name] = consts[name].astype(ml_dtypes.bfloat16)
    for name, value in list({n: inputs[n] for n in _INS}.items()) + list(consts.items()):
        v = np.ascontiguousarray(value)
        arrays[f"in_{name}"] = v
        aps[name] = nc.dram_tensor(f"in_{name}", v.shape, _mybir.dt.from_np(v.dtype), kind="ExternalInput").ap()
    out = nc.dram_tensor("out", (1, SEQ, D), _mybir.dt.float32, kind="ExternalOutput").ap()
    encoder(nc, aps, out)
    r = _run(nc, [arrays], core_ids=[0])
    return r.results[0]["out"]
```
